# Optimizing a Trainium2 kernel written in Bass

```python
import jax, jax.numpy as jnp
from jax import lax
import numpy as np

'''One inference step (4 layers) of a hybrid decoder trunk with parallel gated branches:
branch A = DSA-style sparse GQA attention (lightning indexer + per-query top-k gathered keys,
partial rotary), branch B = LFM2-style gated short convolution; branches merged by per-channel
sigmoid gates, one output projection, DeepNorm post-LayerNorm, squared-ReLU MLP.

Inputs:
  x_prompt    (BATCH, SEQ, D_MODEL)            new sequences; 16 meta tokens prepended inside
  x_sample    (DEC_BATCH, DEC_SEQ, D_MODEL)    new tokens at positions PAST_LEN..PAST_LEN+DEC_SEQ-1
  cache_k     (DEPTH, N_POOL, PAGE_SIZE, N_KV_HEADS, HEAD_DIM)  paged rotary keys
  cache_v     (DEPTH, N_POOL, PAGE_SIZE, N_KV_HEADS, HEAD_DIM)  paged values
  cache_idx_k (DEPTH, N_POOL, PAGE_SIZE, IDX_DIM)               paged indexer keys
  state_conv  (DEPTH, DEC_BATCH, CONV_W-1, CONV_CH)             last gated conv-input rows
  page_table  (DEC_BATCH, N_PAGES) int32, N_PAGES = PAST_LEN // PAGE_SIZE
  weights (stacked over DEPTH) and meta_tokens (N_META, D_MODEL)
Output tuple:
  y_prompt      (BATCH, SEQ, D_MODEL)
  y_sample      (DEC_BATCH, DEC_SEQ, D_MODEL)
  k_prompt      (DEPTH, BATCH, SEQ+N_META, N_KV_HEADS, HEAD_DIM)
  v_prompt      (DEPTH, BATCH, SEQ+N_META, N_KV_HEADS, HEAD_DIM)
  idx_k_prompt  (DEPTH, BATCH, SEQ+N_META, IDX_DIM)
  conv_prompt   (DEPTH, BATCH, CONV_W-1, CONV_CH)
  k_sample      (DEPTH, DEC_BATCH, DEC_SEQ, N_KV_HEADS, HEAD_DIM)
  v_sample      (DEPTH, DEC_BATCH, DEC_SEQ, N_KV_HEADS, HEAD_DIM)
  idx_k_sample  (DEPTH, DEC_BATCH, DEC_SEQ, IDX_DIM)
  conv_sample   (DEPTH, DEC_BATCH, CONV_W-1, CONV_CH)
'''

D_MODEL = 1024
BATCH = 1
SEQ = 512
DEPTH = 2
DEC_BATCH = 8
DEC_SEQ = 4
PAST_LEN = 2048
PAGE_SIZE = 128

N_HEADS = 8
N_KV_HEADS = 2
HEAD_DIM = D_MODEL // N_HEADS
KV_GROUP = N_HEADS // N_KV_HEADS
ROT_DIM = HEAD_DIM // 4
IDX_HEADS = 8
IDX_DIM = 64
IDX_ROT = IDX_DIM // 4
TOPK_MAX = 256
CONV_CH = D_MODEL
CONV_W = 3
D_FF = 4 * D_MODEL
N_META = 16
ROPE_THETA = 500000.0
QBLK = 128
LN_EPS = 1e-5
ALPHA = (2 * DEPTH) ** 0.25
BETA = (8 * DEPTH) ** -0.25
Q_W = N_HEADS * HEAD_DIM
KV_W = N_KV_HEADS * HEAD_DIM
IQ_W = IDX_HEADS * IDX_DIM
SPLITS = (Q_W, KV_W, KV_W, IQ_W, IDX_DIM, IDX_HEADS, CONV_CH, CONV_CH, CONV_CH, D_MODEL, D_MODEL)
P_TOTAL = Q_W + 2 * KV_W + IQ_W + IDX_DIM + IDX_HEADS + 3 * CONV_CH + 2 * D_MODEL

kernel_name = 'dsa_shortconv_gated_hybrid_step'

def _layernorm(x, g, b):
    xf = x.astype(jnp.float32)
    mu = jnp.mean(xf, axis=-1, keepdims=True)
    xc = xf - mu
    var = jnp.mean(jnp.square(xc), axis=-1, keepdims=True)
    y = xc * lax.rsqrt(var + LN_EPS) * g.astype(jnp.float32) + b.astype(jnp.float32)
    return y.astype(x.dtype)

def _rope(x, pos, rot):
    half = rot // 2
    inv = ROPE_THETA ** (-jnp.arange(half, dtype=jnp.float32) * 2.0 / rot)
    ang = pos.astype(jnp.float32)[:, None] * inv[None, :]
    ang = ang.reshape((1, pos.shape[0]) + (1,) * (x.ndim - 3) + (half,))
    cos = jnp.cos(ang).astype(x.dtype)
    sin = jnp.sin(ang).astype(x.dtype)
    x1 = x[..., :half]
    x2 = x[..., half:rot]
    return jnp.concatenate([x1 * cos - x2 * sin, x1 * sin + x2 * cos, x[..., rot:]], axis=-1)

def _project(x, w_in, pos):
    B, T = x.shape[0], x.shape[1]
    z = x @ w_in
    offs = []
    acc = 0
    for w in SPLITS[:-1]:
        acc += w
        offs.append(acc)
    q, k, v, qi, ki, wi, h, bg, cg, ga, gb = jnp.split(z, offs, axis=-1)
    q = _rope(q.reshape(B, T, N_HEADS, HEAD_DIM), pos, ROT_DIM)
    k = _rope(k.reshape(B, T, N_KV_HEADS, HEAD_DIM), pos, ROT_DIM)
    v = v.reshape(B, T, N_KV_HEADS, HEAD_DIM)
    qi = _rope(qi.reshape(B, T, IDX_HEADS, IDX_DIM), pos, IDX_ROT)
    ki = _rope(ki, pos, IDX_ROT)
    wi = wi * (IDX_HEADS ** -0.5)
    u = cg * h
    return q, k, v, qi, ki, wi, u, bg, ga, gb

def _index_scores(qi, ki, wi):
    s = jnp.einsum('bqhd,bld->bqhl', qi, ki).astype(jnp.float32) * (IDX_DIM ** -0.5)
    return jnp.einsum('bqhl,bqh->bql', jax.nn.relu(s), wi.astype(jnp.float32))

def _select(scores, qpos, topk):
    keypos = jnp.arange(scores.shape[-1])
    allowed = keypos[None, :] <= qpos[:, None]
    scores = jnp.where(allowed[None], scores, -jnp.inf)
    _, sel = lax.top_k(scores, topk)
    valid = sel <= qpos[None, :, None]
    return sel, valid

def _gathered_attention(q, kg, vg, valid):
    B, Q = q.shape[0], q.shape[1]
    qg = q.reshape(B, Q, N_KV_HEADS, KV_GROUP, HEAD_DIM)
    logits = jnp.einsum('bqngd,bqjnd->bqngj', qg, kg).astype(jnp.float32) * (HEAD_DIM ** -0.5)
    logits = jnp.where(valid[:, :, None, None, :], logits, -jnp.inf)
    p = jax.nn.softmax(logits, axis=-1).astype(vg.dtype)
    o = jnp.einsum('bqngj,bqjnd->bqngd', p, vg)
    return o.reshape(B, Q, N_HEADS * HEAD_DIM)

def _take_rows(rows, idx):
    return jax.vmap(lambda r, i: r[i])(rows, idx)

def _prompt_attention(q, k, v, qi, ki, wi, topk):
    B, T = q.shape[0], q.shape[1]
    nb = -(-T // QBLK)
    pad = nb * QBLK - T

    def blocks(a):
        a = jnp.pad(a, [(0, 0), (0, pad)] + [(0, 0)] * (a.ndim - 2))
        return a.reshape((B, nb, QBLK) + a.shape[2:]).swapaxes(0, 1)

    qpos = jnp.arange(nb * QBLK).reshape(nb, QBLK)

    def one(args):
        qb, qib, wib, pb = args
        sel, valid = _select(_index_scores(qib, ki, wib), pb, topk)
        return _gathered_attention(qb, _take_rows(k, sel), _take_rows(v, sel), valid)

    o = lax.map(one, (blocks(q), blocks(qi), blocks(wi), qpos))
    return o.swapaxes(0, 1).reshape(B, nb * QBLK, Q_W)[:, :T]

def _sample_attention(q, k_new, v_new, qi, ki_new, wi, pool_k, pool_v, pool_ki, page_table, topk):
    Bd, S = q.shape[0], q.shape[1]
    past = page_table.shape[1] * PAGE_SIZE
    ki_past = pool_ki[page_table].reshape(Bd, past, IDX_DIM)
    ki_all = jnp.concatenate([ki_past, ki_new], axis=1)
    qpos = past + jnp.arange(S)
    sel, valid = _select(_index_scores(qi, ki_all, wi), qpos, topk)
    is_past = (sel < past)[..., None, None]
    sp = jnp.minimum(sel, past - 1)
    phys = jnp.take_along_axis(page_table, (sp // PAGE_SIZE).reshape(Bd, -1), axis=1).reshape(sp.shape)
    off = sp % PAGE_SIZE
    sn = jnp.clip(sel - past, 0, S - 1)
    kg = jnp.where(is_past, pool_k[phys, off], _take_rows(k_new, sn))
    vg = jnp.where(is_past, pool_v[phys, off], _take_rows(v_new, sn))
    return _gathered_attention(q, kg, vg, valid)

def _short_conv(u, past, conv_w):
    T = u.shape[1]
    up = jnp.concatenate([past, u], axis=1)
    y = conv_w[0] * up[:, 0:T]
    for j in range(1, CONV_W):
        y = y + conv_w[j] * up[:, j:j + T]
    return y, up[:, -(CONV_W - 1):]

def _merge_and_ffn(x, attn, cy, bg, ga, gb, w_oa, w_ob, w_o, ln1_g, ln1_b, w_up, w_down, ln2_g, ln2_b):
    branch_a = attn @ w_oa
    branch_b = (bg * cy) @ w_ob
    mix = (jax.nn.sigmoid(ga) * branch_a + jax.nn.sigmoid(gb) * branch_b) @ w_o
    x = _layernorm(ALPHA * x + mix, ln1_g, ln1_b)
    hdn = jnp.square(jax.nn.relu(x @ w_up))
    return _layernorm(ALPHA * x + hdn @ w_down, ln2_g, ln2_b)

def setup_inputs(seed: int = 0) -> dict:
    key = jax.random.key(seed)
    ks = jax.random.split(key, 24)
    n_pages = PAST_LEN // PAGE_SIZE
    n_pool = (DEC_BATCH * n_pages * 5) // 4
    f32 = jnp.float32
    nrm = lambda k, s: jax.random.normal(k, s, f32)
    perm = jax.random.permutation(ks[0], n_pool)[:DEC_BATCH * n_pages]
    return {
        'x_prompt': nrm(ks[1], (BATCH, SEQ, D_MODEL)),
        'x_sample': nrm(ks[2], (DEC_BATCH, DEC_SEQ, D_MODEL)),
        'cache_k': nrm(ks[3], (DEPTH, n_pool, PAGE_SIZE, N_KV_HEADS, HEAD_DIM)),
        'cache_v': nrm(ks[4], (DEPTH, n_pool, PAGE_SIZE, N_KV_HEADS, HEAD_DIM)),
        'cache_idx_k': nrm(ks[5], (DEPTH, n_pool, PAGE_SIZE, IDX_DIM)),
        'state_conv': nrm(ks[6], (DEPTH, DEC_BATCH, CONV_W - 1, CONV_CH)),
        'page_table': perm.reshape(DEC_BATCH, n_pages).astype(jnp.int32),
        'meta_tokens': nrm(ks[7], (N_META, D_MODEL)),
        'w_in': nrm(ks[8], (DEPTH, D_MODEL, P_TOTAL)) * D_MODEL ** -0.5,
        'conv_w': nrm(ks[9], (DEPTH, CONV_W, CONV_CH)) * CONV_W ** -0.5,
        'w_attn_out': nrm(ks[10], (DEPTH, Q_W, D_MODEL)) * Q_W ** -0.5,
        'w_conv_out': nrm(ks[11], (DEPTH, CONV_CH, D_MODEL)) * CONV_CH ** -0.5,
        'w_o': nrm(ks[12], (DEPTH, D_MODEL, D_MODEL)) * (D_MODEL ** -0.5 * BETA),
        'ln1_g': 1.0 + 0.02 * nrm(ks[13], (DEPTH, D_MODEL)),
        'ln1_b': 0.02 * nrm(ks[14], (DEPTH, D_MODEL)),
        'w_up': nrm(ks[15], (DEPTH, D_MODEL, D_FF)) * D_MODEL ** -0.5,
        'w_down': nrm(ks[16], (DEPTH, D_FF, D_MODEL)) * (D_FF ** -0.5 * BETA),
        'ln2_g': 1.0 + 0.02 * nrm(ks[17], (DEPTH, D_MODEL)),
        'ln2_b': 0.02 * nrm(ks[18], (DEPTH, D_MODEL)),
    }

def reference(x_prompt, x_sample, cache_k, cache_v, cache_idx_k, state_conv, page_table, meta_tokens,
              w_in, conv_w, w_attn_out, w_conv_out, w_o, ln1_g, ln1_b, w_up, w_down, ln2_g, ln2_b):
    B = x_prompt.shape[0]
    S = x_sample.shape[1]
    past = page_table.shape[1] * PAGE_SIZE
    meta = jnp.broadcast_to(meta_tokens.astype(x_prompt.dtype)[None], (B, N_META, D_MODEL))
    xp = jnp.concatenate([meta, x_prompt], axis=1)
    xs = x_sample
    pos_p = jnp.arange(xp.shape[1])
    pos_s = past + jnp.arange(S)
    topk_p = min(TOPK_MAX, x_prompt.shape[1] // 4)
    topk_s = min(TOPK_MAX, (past + S) // 4)
    zero_past = jnp.zeros((B, CONV_W - 1, CONV_CH), xp.dtype)
    kp, vp, kip, cp, ksl, vsl, kisl, csl = [], [], [], [], [], [], [], []
    for l in range(DEPTH):
        lw = (w_attn_out[l], w_conv_out[l], w_o[l], ln1_g[l], ln1_b[l], w_up[l], w_down[l], ln2_g[l], ln2_b[l])
        q, k, v, qi, ki, wi, u, bg, ga, gb = _project(xp, w_in[l], pos_p)
        attn = _prompt_attention(q, k, v, qi, ki, wi, topk_p)
        cy, cstate = _short_conv(u, zero_past, conv_w[l])
        xp = _merge_and_ffn(xp, attn, cy, bg, ga, gb, *lw)
        kp.append(k)
        vp.append(v)
        kip.append(ki)
        cp.append(cstate)
        q, k, v, qi, ki, wi, u, bg, ga, gb = _project(xs, w_in[l], pos_s)
        attn = _sample_attention(q, k, v, qi, ki, wi, cache_k[l], cache_v[l], cache_idx_k[l], page_table, topk_s)
        cy, cstate = _short_conv(u, state_conv[l].astype(u.dtype), conv_w[l])
        xs = _merge_and_ffn(xs, attn, cy, bg, ga, gb, *lw)
        ksl.append(k)
        vsl.append(v)
        kisl.append(ki)
        csl.append(cstate)
    y_prompt = xp[:, N_META:]
    return (y_prompt, xs, jnp.stack(kp), jnp.stack(vp), jnp.stack(kip), jnp.stack(cp),
            jnp.stack(ksl), jnp.stack(vsl), jnp.stack(kisl), jnp.stack(csl))


_drawn_inputs = setup_inputs


def setup_inputs(seed=0):
    import zlib

    import numpy as np

    out = dict(_drawn_inputs(seed))
    spreads = {}
    factors = {}
    for name, (base, spread) in spreads.items():
        noise = np.random.default_rng([zlib.crc32(name.encode()), seed]).standard_normal(out[name].shape)
        drawn = base * np.exp(spread * noise) if base else spread * noise
        out[name] = __import__('jax').numpy.asarray(drawn.astype(out[name].dtype))
    for name, factor in factors.items():
        out[name] = (out[name] * factor).astype(out[name].dtype)
    return out
```

```python
from contextlib import ExitStack, contextmanager

import concourse.bass as bass
from concourse import mybir

F32 = mybir.dt.float32
F32R = mybir.dt.float32r
BF16 = mybir.dt.bfloat16
I32 = mybir.dt.int32
U32 = mybir.dt.uint32
ACT = mybir.ActivationFunctionType
ALU = mybir.AluOpType
AX_X = mybir.AxisListType.X

P = 128
DM = 1024
KC = DM // P
DEPTH = 2
SEQ, N_META = 512, 16
RP = SEQ + N_META
NB, NS = 8, 4
RS = NB * NS
R = RP + RS
RH = R // 2
HEADS, KVH, HD = 8, 2, 128
GRP = HEADS // KVH
IH, ID = 8, 64
ROT, IDX_ROT = HD // 4, ID // 4
LAYER_LINKS, PAIR_LINKS = 384, 46
KV_W = KVH * HD
PAST, PAGE = 2048, 128
NPG = PAST // PAGE
TPP = PAST // P
KEYS_S = PAST + RS
TOPK_P, TOPK_S = SEQ // 4, 256
CW = 3
DFF = 4096
NG = DFF // DM
P_TOTAL = 7240
COL_Q, COL_K, COL_V, COL_QI, COL_KI = 0, 1024, 1280, 1536, 2048
COL_H, COL_BG, COL_CG, COL_GA, COL_GB = 2120, 3144, 4168, 5192, 6216
UE_W = 2 + RP + NB * (2 + NS)
ALPHA = float((2 * DEPTH) ** 0.25)
EPS = 1e-5
SC_HD = float(HD) ** -0.5
SC_WI = float(IH) ** -0.5 * float(ID) ** -0.5
NEG_KEY = -3.0e38
NEG_TAKEN = -3.3e38
NEG_CUT = -3.2e38
NEG_MASK = -1.0e30
TILES = [(0, 128), (128, 128), (256, 128), (384, 128), (512, 16), (528, 32)]
PTILES = TILES[:5]
KW = [min(c + 128, RP) for c, _ in PTILES]

USES = (73, 72)
CONV, AO, WO, UP = 5, 6, 7, 8
GATES = ("h", "cg", "bg", "ga", "gb")


def phase_use(s, ph):
    return (9, 8)[s] + 4 * ph


def gate_use(s, k):
    return (9, 8)[s] + k // 2


def apart(eng, started):
    eng.sem_inc(started, 1)


class Chain:

    def __init__(self, eng, sem, started):
        self.eng, self.sem, self.started, self.base, self.k = eng, sem, started, 0, 0

    def link(self, ins, alone=False):
        ins.then_inc(self.sem, 1)
        self.k += 1
        self.eng.wait_ge(self.sem, self.base + self.k)
        if alone:
            apart(self.eng, self.started)

    @contextmanager
    def fori(self, n, per):
        apart(self.eng, self.started)
        with self.eng.Fori(0, n) as i:
            base, k = self.base, self.k
            self.base, self.k = base + k + i * per, 0
            yield i
            assert self.k == per, (self.k, per)
        self.base, self.k = base, k + n * per


def trunk_program(nc, a):
    with ExitStack() as ctx:
        def sb(name, shape, dt):
            return ctx.enter_context(nc.sbuf_tensor(name, shape, dt))

        def arena(name, nbytes):
            off = (nc.sbuf_base + 31) // 32 * 32
            sb(name, [P, nbytes // 4], F32)
            return off

        def at(name, shape, dt, off):
            return nc.alloc_sbuf_tensor_at(name, shape, dt, offset=off)

        BIG = KC * R * 4
        X = sb("X", [P, KC, R], F32)
        off_axh, off_axl, off_ahh, off_ahl = (arena(n, BIG) for n in ("r_axh", "r_axl", "r_ahh", "r_ahl"))
        AXh, AXl = at("AXh", [P, KC, R], F32R, off_axh), at("AXl", [P, KC, R], F32R, off_axl)
        AHh, AHl = at("AHh", [P, KC, R], F32R, off_ahh), at("AHl", [P, KC, R], F32R, off_ahl)
        KVB = [[at(f"KVB{h}{b4}", [P, TPP // 2, KV_W], F32, (off_axh, off_axl, off_ahh, off_ahl)[2 * h + b4 // 2]
                   + b4 % 2 * (TPP // 2 * KV_W * 4)) for b4 in range(4)] for h in range(2)]
        IKB = [at(f"IKB{g}", [P, 4, TPP, ID], F32, o) for g, o in enumerate((off_ahh, off_ahl))]
        RELU_S = [at(f"RELU_S{g}", [P, KEYS_S], F32, o) for g, o in enumerate((off_ahh, off_ahl))]
        off_q = arena("r_q", BIG)
        Q = at("Q", [P, KC, R], F32, off_q)
        SD = at("SD", [P, R], F32, off_q)
        RSTD = at("RSTD", [P, R], F32, off_q + 4 * R)
        off_sg = arena("r_sg", BIG)
        SG = at("SG", [P, KC, R], F32, off_sg)
        QI = at("QI", [P, 4, R], F32, off_sg)
        KIT = [at(f"KIT{i}", [P, 512], F32, off_sg + 4 * 4 * R + i * 2048) for i in range(4)]
        SQ = at("SQ", [P, KC, R], F32, off_sg)
        off_bb = arena("r_bb", BIG)
        BB = at("BB", [P, KC, R], F32, off_bb)
        TK, o = [None], off_bb
        for r in range(1, 5):
            TK.append(at(f"TK{r}", [P, KW[r]], F32, o))
            o += 4 * KW[r]
        KNS = [at(f"KNS{i}", [P, KV_W], F32, o + 1024 * i) for i in range(2)]
        RELU_P = [at(f"RELU_P{i}", [P, RP], F32, o + 2048 + 2112 * i) for i in range(2)]
        ROPE = at("ROPE", [P, R], F32, o + 2048 + 4224)
        off_u = arena("r_u", 14528)
        UE = at("UE", [P, UE_W], F32, off_u)
        CY = at("CY", [P, R], F32, off_u + 2336)
        ICOS, ISIN = at("ICOS", [P, R], F32, off_u), at("ISIN", [P, R], F32, off_u + 2240)
        QCOS, QSIN = at("QCOS", [32, R], F32, off_u + 4480), at("QSIN", [32, R], F32, off_u + 6720)
        KI, KD = at("KI", [P, R], F32, off_u + 8960), at("KD", [P, R], F32, off_u + 11200)
        QS = at("QS", [P, NB, IH, NS], F32, off_u + 13440)
        QST = at("QST", [P, RP], F32, off_u + 4576)
        PP = [at(f"PP{i}", [P, RP], F32, off_u + 6688 + 2112 * i) for i in range(2)]
        PPT = at("PPT", [P, 512], F32, off_u + 10912)
        MS = at("MS", [RS, KEYS_S], BF16, off_u)
        QP = at("QP", [P, NB, KVH, HEADS, NS], F32, off_u + 4160)
        KTR = [at(f"KTR{i}", [P, 512], F32, off_u + 6208 + 2048 * i) for i in range(4)]
        MT = [at(f"MT{i}", [P, R], F32, off_u + 2240 * i) for i in range(4)]
        NAT = [at(f"NAT{i}", [P, DM], F32, off_u + 4096 * i) for i in range(2)]
        ST = [sb(f"ST{s}", [P, KC, P], F32) for s in range(2)]
        WH = [sb(f"WH{s}", [P, KC, P], F32R) for s in range(2)]
        WL = [sb(f"WL{s}", [P, KC, P], F32R) for s in range(2)]
        KT = sb("KT", [P, KVH, R], F32)
        VN = sb("VN", [P, 6, KV_W], F32)
        off_m = arena("r_m", 2 * sum(KW[1:]) + 4 * KEYS_S)
        MP, o = [None], off_m
        for r in range(1, 5):
            MP.append(at(f"MP{r}", [P, KW[r]], BF16, o))
            o += 2 * KW[r]
        TKS = at("TKS", [RS, KEYS_S], F32, o)
        PS_S = at("PS_S", [P, KEYS_S], F32, off_m)
        O_S = at("O_S", [P, KV_W], F32, off_m + 8320)
        VT = at("VT", [P, KVH, R], F32, off_m)
        PALL = at("PALL", [P, P], F32, off_m + 1024)
        SCN = at("SCN", [P, P], F32, off_m + 2 * 4 * R)
        SELF = at("SELF", [RS, 2, P], F32, off_m)
        off_w = arena("r_w", 6 * (ID + IH) * 4)
        WKN = at("WKN", [P, 6, ID + IH], F32, off_w)
        CSN = at("CSN", [P, 2, P], F32, off_w)
        ident = sb("ident", [P, P], F32)
        identb = sb("identb", [P, P], BF16)
        caus = sb("caus", [P, P], F32)
        causb = sb("causb", [P, P], BF16)
        ones = sb("ones", [P, P], F32)
        selb = sb("selb", [RS, 2, P], BF16)
        expand = sb("expand", [P, P], F32)
        pick = sb("pick", [P, 2, RS], F32)
        newok = sb("newok", [RS, RS], F32)
        PTT = sb("PTT", [P, 112], F32)
        PL = sb("PL", [P, 56], F32)
        SCT = sb("SCT", [P, P], F32)
        CSO = sb("CSO", [P, 18, KC], F32)
        WIB = sb("WIB", [P, 2, RS], F32)
        PTB = sb("PTB", [P, NB], I32)
        SEG = sb("SEG", [P, 1], F32)
        IDX = sb("IDX", [P, NB], U32)
        IDXH = sb("IDXH", [P, 2, NB], U32)
        top = sb("top", [P, 4, 8], F32)
        st = sb("st", [P, 16], F32)
        stp = sb("stp", [P, 2, 4], F32)
        eps = sb("eps", [P, 1], F32)
        PS = [ctx.enter_context(nc.psum_tensor(f"PS{s}", [P, 2, 512], F32)) for s in range(2)]
        PB = ctx.enter_context(nc.psum_tensor("PB", [P, 4, 512], F32))

        def sem(name):
            return ctx.enter_context(nc.semaphore(name))

        loaded = [sem(f"loaded{s}") for s in range(2)]
        hi_done = [sem(f"hi_done{s}") for s in range(2)]
        lo_done = [sem(f"lo_done{s}") for s in range(2)]
        mm_done = [sem(f"mm_done{s}") for s in range(2)]
        evac_done = [sem(f"evac_done{s}") for s in range(2)]
        started = sem("started")
        a_ready = sem("a_ready")
        dve_own = sem("dve_own")
        const_in, x_in = sem("const_in"), [sem(f"x_in{i}") for i in range(2)]
        setup_t, setup_e = sem("setup_t"), sem("setup_e")
        params_t = sem("params_t")
        idx_ready, tables_in, state_in, ik_in = sem("idx_ready"), sem("tables_in"), sem("state_in"), sem("ik_in")
        qi_roped, ki_ready, kv_ready, q_ready = sem("qi_roped"), sem("ki_ready"), sem("kv_ready"), sem("q_ready")
        ki_t, ki_e, wi_mm, wib_ready = sem("ki_t"), sem("ki_e"), sem("wi_mm"), sem("wib_ready")
        kv_t, kv_e = sem("kv_t"), sem("kv_e")
        out_small = sem("out_small")
        out_k, out_v = [sem(f"out_k{i}") for i in range(2)], sem("out_v")
        sc_mm, sc_relu, sc_acc = sem("sc_mm"), sem("sc_relu"), sem("sc_acc")
        kit_t, kit_e, ss_step, ss_mm, ss_relu = (sem("kit_t"), sem("kit_e"), sem("ss_step"), sem("ss_mm"),
                                                 sem("ss_relu"))
        w_mm, tks_ready, ue_init = sem("w_mm"), sem("tks_ready"), sem("ue_init")
        cso_ready, cso_t, cso_e, out_c = sem("cso_ready"), sem("cso_t"), sem("cso_e"), sem("out_c")
        mp_ready = sem("mp_ready")
        masks_ready, qp_ready = sem("masks_ready"), sem("qp_ready")
        kv_in = [[sem(f"kv_in{h}{b4}") for b4 in range(4)] for h in range(2)]
        kt_t, kt_ea, kt_ed, kt_mm = sem("kt_t"), sem("kt_ea"), sem("kt_ed"), sem("kt_mm")
        ls_mm, ls_max, ls_exp = sem("ls_mm"), sem("ls_max"), sem("ls_exp")
        pt_t, pt_e, pv_mm, os_e, ot_t, ot_e = (sem("pt_t"), sem("pt_e"), sem("pv_mm"), sem("os_e"),
                                               sem("ot_t"), sem("ot_e"))
        qst_done, lp_mm, lp_max = sem("qst_done"), sem("lp_mm"), sem("lp_max")
        lp_exp, pp_norm = sem("lp_exp"), sem("pp_norm")
        pp_t, pp_e, op_mm, op_e = sem("pp_t"), sem("pp_e"), sem("op_mm"), sem("op_e")
        relu_h = sem("relu_h")
        ln_sum, ln_dev, ln_sq, ln_var, ln_sd, ln_norm, ln_aff = (sem("ln_sum"), sem("ln_dev"), sem("ln_sq"),
                                                                sem("ln_var"), sem("ln_sd"), sem("ln_norm"), sem("ln_aff"))
        y_t, y_e, out_y = sem("y_t"), sem("y_e"), [sem(f"out_y{i}") for i in range(2)]

        block = ctx.enter_context(nc.Block())

        w_in_v = a["w_in"].rearrange("l (c p) n -> l p c n", p=P)
        w_views = {n: a[n].rearrange("l (c p) n -> l p c n", p=P) for n in ("w_attn_out", "w_conv_out", "w_o", "w_up")}
        w_down_v = a["w_down"].rearrange("l (g c p) n -> (l g) p c n", g=NG, p=P)
        rows_k = a["cache_k"].rearrange("l n (s t) h d -> (l n s) (t h d)", t=TPP // 2)
        rows_v = a["cache_v"].rearrange("l n (s t) h d -> (l n s) (t h d)", t=TPP // 2)
        rows_ik = a["cache_idx_k"].rearrange("l n (s t) d -> (l n s) (t d)", t=TPP)
        n_rows = a["cache_k"].shape[1] * (PAGE // TPP)

        def rope_swap(half):
            return [(j + half) % (2 * half) if j < 2 * half else j for j in range(32)]

        @block.sync
        def _(sp):
            def load(s, n, src):
                sp.wait_ge(lo_done[s], n + 1)
                sp.dma_start(ST[s][:, :, :], src).then_inc(loaded[s], 16)

            def wcol(v, l, col):
                return v[bass.ds(l, 1), :, :, bass.ds(col, P)].rearrange("o p c n -> (o p) c n")

            with nc.allow_non_contiguous_dma(reason="page ids, one word each"):
                for j in range(NPG):
                    sp.dma_start(PTB[8 * j:8 * j + 8, :],
                                 a["page_table"][:, j:j + 1].rearrange("b j -> j b").to_broadcast([8, NB])
                                 ).then_inc(const_in, 16)
            for t, n in ((ident, "c_ident"), (caus, "c_caus"), (expand, "c_expand"), (pick, "c_pick"),
                         (newok, "c_newok"), (SEG, "c_seg"), (SELF, "c_sel")):
                sp.dma_start(t[:], a[n]).then_inc(const_in, 16)
            for l in range(DEPTH):
                for j, n in enumerate(("ln1_g", "ln1_b", "ln2_g", "ln2_b")):
                    sp.dma_start(PALL[56 * l + 8 * j:56 * l + 8 * j + 8, :],
                                 a[n][l].rearrange("(c d) -> c d", d=P)).then_inc(const_in, 16)
                sp.dma_start(PALL[56 * l + 32:56 * l + 56, :],
                             a["conv_w"][l].rearrange("j (c d) -> (j c) d", d=P)).then_inc(const_in, 16)
            for s in range(2):
                load(s, 0, w_in_v[0, :, :, COL_QI + P * s:COL_QI + P * s + P])
            srcs = [(a["meta_tokens"], 16)] + [(a["x_prompt"][0, P * t:P * t + P, :], P) for t in range(4)]
            srcs += [(a["x_sample"].rearrange("b s d -> (b s) d"), RS)]
            for t, (src, n) in enumerate(srcs):
                if t >= 2:
                    sp.wait_ge(setup_t, t - 1)
                sp.dma_start(NAT[t % 2][0:n, :], src).then_inc(x_in[t % 2], 16)

            with sp.Fori(0, DEPTH) as l:
                def use(s, n):
                    return l * USES[s] + n

                load(0, use(0, 1), wcol(w_in_v, l, COL_QI + 2 * P))
                load(1, use(1, 1), wcol(w_in_v, l, COL_QI + 3 * P))
                load(0, use(0, 2), wcol(w_in_v, l, COL_KI))
                load(1, use(1, 2), wcol(w_in_v, l, COL_K + P))
                load(0, use(0, 3), wcol(w_in_v, l, COL_K))
                load(0, use(0, 4), wcol(w_in_v, l, COL_V))
                load(1, use(1, 3), wcol(w_in_v, l, COL_V + P))
                with sp.Fori(0, 4) as i:
                    for s in range(2):
                        load(s, l * USES[s] + (phase_use(s, -1) + i), wcol(w_in_v, l, COL_Q + s * P + i * (2 * P)))
                with sp.Fori(0, KC // 2) as i:
                    for k in range(10):
                        col = (COL_H, COL_CG, COL_BG, COL_GA, COL_GB)[k % 5] + P * (k // 5)
                        load(k % 2, l * USES[k % 2] + i * 5 + gate_use(k % 2, k), wcol(w_in_v, l, i * (2 * P) + col))
                for name, ph in (("w_conv_out", CONV), ("w_attn_out", AO), ("w_o", WO)):
                    with sp.Fori(0, 4) as i:
                        for s in range(2):
                            load(s, l * USES[s] + (phase_use(s, ph) + i), wcol(w_views[name], l, s * P + i * (2 * P)))
                with sp.Fori(0, NG) as g:
                    with sp.Fori(0, 4) as i:
                        for s in range(2):
                            load(s, l * USES[s] + g * 8 + i + phase_use(s, 8),
                                 wcol(w_views["w_up"], l, g * DM + i * (2 * P) + s * P))
                    with sp.Fori(0, 4) as i:
                        for s in range(2):
                            load(s, l * USES[s] + g * 8 + i + phase_use(s, 9),
                                 wcol(w_down_v, l * NG + g, i * (2 * P) + s * P))
                for s in range(2):
                    load(s, use(s, USES[s]), wcol(w_in_v, (l + 1) % DEPTH, COL_QI + P * s))
            for s in range(2):
                sp.wait_ge(loaded[s], 16 * (DEPTH * USES[s] + 1))

        @block.gpsimd
        def _(pool):
            def rest(s, n):
                pool.wait_ge(hi_done[s], n + 1)
                pool.tensor_tensor(WL[s][:, :, :], ST[s][:, :, :], WH[s][:, :, :].bitcast(F32),
                                   ALU.subtract).then_inc(lo_done[s], 1)

            for s in range(2):
                pool.sem_inc(lo_done[s], 1)
            for s in range(2):
                rest(s, 0)
            with pool.Fori(0, DEPTH) as l:
                pool.wait_ge(a_ready, l * 72 + 8)
                apart(pool, started)
                for n, t in (("c_icos", ICOS), ("c_isin", ISIN), ("c_qcos", QCOS), ("c_qsin", QSIN)):
                    pool.dma_start(t[:, :], a[n]).then_inc(tables_in, 16)
                pool.dma_start(SCN[:, :], a["state_conv"][bass.ds(l, 1)].rearrange("o b t (c d) -> (o b t c) d", d=P)
                               ).then_inc(state_in, 16)
                pool.wait_ge(idx_ready, l + 1)
                apart(pool, started)
                for b in range(NB):
                    pool.indirect_dma_start(IKB[b // 4][:, b % 4].rearrange("p t d -> p (t d)"), None, rows_ik,
                                            bass.IndirectOffsetOnAxis(ap=IDX[:, b:b + 1], axis=0)
                                            ).then_inc(ik_in, 16)
                for s, n in ((0, 1), (1, 1), (0, 2), (1, 2), (0, 3), (0, 4), (1, 3)):
                    rest(s, l * USES[s] + n)
                with pool.Fori(0, 4 * (CONV + 1)) as i:
                    for s in range(2):
                        rest(s, l * USES[s] + i + phase_use(s, -1))
                for s in range(2):
                    rest(s, l * USES[s] + phase_use(s, CONV))

                def gather(g, h, rows):
                    for b4 in range(4):
                        b = 4 * g + b4
                        pool.indirect_dma_start(KVB[h][b4][:].rearrange("p t d -> p (t d)"), None, rows,
                                                bass.IndirectOffsetOnAxis(ap=IDXH[:, h, b:b + 1], axis=0)
                                                ).then_inc(kv_in[h][b4], 16)

                def products_done(ph):
                    for s in range(2):
                        pool.wait_ge(mm_done[s], l * USES[s] + phase_use(s, ph) + 1)
                        apart(pool, started)

                products_done(CONV)
                gather(0, 0, rows_k)
                with pool.Fori(0, 3) as i:
                    for s in range(2):
                        rest(s, l * USES[s] + i + (phase_use(s, CONV) + 1))
                for s in range(2):
                    rest(s, l * USES[s] + phase_use(s, AO))
                products_done(AO)
                gather(0, 1, rows_k)
                for g in range(2):
                    if g == 1:
                        for h in range(2):
                            pool.wait_ge(pv_mm, l * 10 + 2 * h + 2)
                            apart(pool, started)
                            gather(1, h, rows_k)
                    for h in range(2):
                        pool.wait_ge(kt_t, l * 64 + 32 * g + 16 * h + 16)
                        apart(pool, started)
                        gather(g, h, rows_v)
                with pool.Fori(0, 3) as i:
                    for s in range(2):
                        rest(s, l * USES[s] + i + (phase_use(s, 6) + 1))
                with pool.Fori(0, 4 + 4 * 2 * NG) as i:
                    for s in range(2):
                        rest(s, l * USES[s] + i + phase_use(s, 7))
                for s in range(2):
                    rest(s, l * USES[s] + USES[s])

        @block.tensor
        def _(pe):
            for s in range(2):
                pe.sem_inc(mm_done[s], 1)

            def unit(s, n, hi, lo, ready=None, first=True, last=True):
                pe.wait_ge(lo_done[s], n + 2)
                pe.wait_ge(evac_done[s], n + 1)
                for k in range(KC):
                    if ready is not None:
                        pe.wait_ge(a_ready, ready + k)
                    for x, y in ((WH[s], hi), (WL[s], hi), (WH[s], lo)):
                        for h in range(2):
                            mm = pe.matmul(PS[s][:, h, 0:RH], x[:, k, :], y[:, k, RH * h:RH * h + RH],
                                           start=(k == 0 and y is hi and x is WH[s]),
                                           stop=(k == KC - 1 and y is lo))
                mm.then_inc(mm_done[s], 1)

            pe.wait_ge(const_in, 16 * (NPG + 7 + 10))
            for t, (c0, n) in enumerate([(0, 16)] + [(16 + P * j, P) for j in range(4)] + [(RP, RS)]):
                pe.wait_ge(x_in[t % 2], 16 * (t // 2 + 1))
                if t >= 2:
                    pe.wait_ge(setup_e, t - 1)
                for c in range(KC):
                    tr = pe.transpose(PS[t % 2][:, c // 4, P * (c % 4):P * (c % 4) + n],
                                      NAT[t % 2][0:n, P * c:P * c + P], ident[0:n, 0:n])
                tr.then_inc(setup_t, 1)
            pe.transpose(PB[:, 0, 0:112], PALL[0:112, :], ident[0:112, 0:112]).then_inc(params_t, 1)
            pe.wait_ge(setup_e, 6)

            apart(pe, started)
            with pe.Fori(0, DEPTH) as l:
                def use(s, n):
                    return l * USES[s] + n

                x0 = l * 72 + 1
                for s, n in ((0, 0), (1, 0), (0, 1), (1, 1), (0, 2), (0, 3), (1, 2), (0, 4), (1, 3)):
                    unit(s, use(s, n), AXh, AXl, ready=x0 if n == 0 else None)
                apart(pe, started)
                with pe.Fori(0, 4) as i:
                    for s in range(2):
                        unit(s, l * USES[s] + i + phase_use(s, -1), AXh, AXl)

                pe.wait_ge(ki_ready, l + 1)
                apart(pe, started)
                for t, (c0, n) in enumerate(TILES):
                    tr = pe.transpose(PB[0:n, 0, 80 * t:80 * t + 72], KI[0:72, c0:c0 + n], ident[0:72, 0:72])
                tr.then_inc(ki_t, 1)
                pe.matmul(PB[:, 1, 0:RS], expand[ID:ID + IH, :], KI[ID:ID + IH, RP:R], start=True, stop=True)
                pe.wait_ge(state_in, l * 16 + 16)
                pe.transpose(PB[:, 1, P:2 * P], SCN[:, :], ident[:, :]).then_inc(wi_mm, 1)
                pe.wait_ge(kv_ready, l + 1)
                pe.wait_ge(evac_done[1], use(1, 4) + 1)
                pe.wait_ge(evac_done[0], use(0, 5) + 1)
                for t, (c0, n) in enumerate(TILES):
                    if t >= 2:
                        pe.wait_ge(kv_e, l * 6 + t - 1)
                    for h in range(KVH):
                        pe.transpose(PB[0:n, 2 + t % 2, P * h:P * h + P], KT[:, h, c0:c0 + n], ident[:, :])
                        tr = pe.transpose(PB[0:n, 2 + t % 2, 256 + P * h:256 + P * h + P], VT[:, h, c0:c0 + n],
                                          ident[:, :])
                    tr.then_inc(kv_t, 1)

                pe.wait_ge(qi_roped, l + 1)
                for s in range(2):
                    pe.wait_ge(evac_done[s], use(s, (9, 8)[s]) + 1)
                j = 0
                for r in range(1, 5):
                    c0, n = PTILES[r]
                    for h in range(IH):
                        if j >= 2:
                            pe.wait_ge(sc_relu, l * 32 + j - 1)
                            apart(pe, started)
                        hp = ID * (h % 2)
                        for k0 in range(0, KW[r], 512):
                            k1 = min(k0 + 512, KW[r])
                            mm = pe.matmul(PS[j % 2][0:n, k0 // 512, 0:k1 - k0], QI[hp:hp + ID, h // 2, c0:c0 + n],
                                           KD[hp:hp + ID, k0:k1], start=True, stop=True)
                        mm.then_inc(sc_mm, 1)
                        j += 1

                pe.wait_ge(ik_in, (l + 1) * (16 * NB))
                pe.wait_ge(ki_e, l + 1)
                pe.wait_ge(wib_ready, l + 1)
                pe.wait_ge(kv_e, l * 6 + 6)
                pe.wait_ge(sc_relu, l * 32 + 32)

                def ik_transposes(t):
                    g, jh, j = t // 8, t // 4 % 2, t % 4
                    if t >= 4:
                        pe.wait_ge(kit_e, l * 16 + t - 3)
                    for i in range(4):
                        tok = 8 * jh + 2 * i
                        tr = pe.transpose(PB[:, j, P * i:P * i + P],
                                          IKB[g][:, j, tok:tok + 2, :].rearrange("p t d -> p (t d)"), ident[:, :])
                    tr.then_inc(kit_t, 1)

                for t in range(4):
                    ik_transposes(t)
                for q in range(4):
                    g, jh = q // 2, q % 2
                    pe.wait_ge(kit_e, l * 16 + 4 * q + 4)
                    apart(pe, started)
                    if q == 2:
                        pe.wait_ge(ss_relu, l * 3 + 1)
                        apart(pe, started)
                    for par in range(2):
                        for j in range(4):
                            mm = pe.matmul(PS[par][32 * j:32 * j + 32, jh, :],
                                           QS[ID * par:ID * par + ID, 4 * g + j].rearrange("p h s -> p (h s)"),
                                           KIT[j][ID * par:ID * par + ID, :], start=True, stop=True)
                    mm.then_inc(ss_step, 1)
                    if q < 3:
                        for t in range(4 * q + 4, 4 * q + 8):
                            ik_transposes(t)
                for b in range(NB):
                    b4 = 32 * (b % 4)
                    mm = pe.matmul(PB[b4:b4 + 32, 0, 32 * (b // 4):32 * (b // 4) + 32],
                                   QS[0:ID, b].rearrange("p h s -> p (h s)"), KD[0:ID, RP:R], start=True, stop=True)
                mm.then_inc(ss_mm, 1)
                pe.wait_ge(ss_relu, l * 3 + 3)
                apart(pe, started)
                for par in range(2):
                    for jh in range(2):
                        col = 512 * (2 * par + jh)
                        for g in range(2):
                            pe.matmul(PS[par][0:RS, jh, :], WIB[:, g, :], RELU_S[g][:, col:col + 512],
                                      start=(g == 0), stop=(g == 1))
                for g in range(2):
                    mm = pe.matmul(PB[0:RS, 1, 0:RS], WIB[:, g, :], RELU_S[g][:, PAST:KEYS_S],
                                   start=(g == 0), stop=(g == 1))
                mm.then_inc(w_mm, 1)

                pe.wait_ge(tks_ready, l + 1)
                pe.wait_ge(mp_ready, l + 1)
                for n in range(KVH):
                    apart(pe, started)
                    with pe.Fori(0, GRP // 2) as i2:
                        pair = i2 + 2 * n
                        for hb in range(2):
                            H = l * HEADS + pair * 2 + hb

                            def gate(k):
                                k += 5 * hb
                                unit(k % 2, l * USES[k % 2] + pair * 5 + gate_use(k % 2, k), AXh, AXl)

                            def p_logits(r):
                                c0, m = PTILES[r]
                                pe.wait_ge(lp_exp, H * 5 + r + (2 if r in (0, 4) else 1))
                                apart(pe, started)
                                msk = causb if r == 0 else MP[r]
                                for k0 in range(0, KW[r], 512):
                                    k1 = min(k0 + 512, KW[r])
                                    bank = PB[0:m, (r + k0 // 512) % 2, 0:k1 - k0]
                                    pe.matmul(bank, identb[0:m, 0:m], msk[0:m, k0:k1], start=True, stop=False)
                                    mm = pe.matmul(bank, QST[:, c0:c0 + m], KT[:, n, k0:k1], start=False, stop=True)
                                mm.then_inc(lp_mm, 1)

                            def p_transposes(r):
                                m = PTILES[r][1]
                                pe.wait_ge(pp_norm, H * 5 + r + 1)
                                apart(pe, started)
                                for kt in range((KW[r] + P - 1) // P):
                                    k1 = min(P, KW[r] - P * kt)
                                    tr = pe.transpose(PB[0:k1, 2, m * kt:m * kt + m], PP[r % 2][0:m, P * kt:P * kt + k1],
                                                      ident[0:m, 0:m])
                                tr.then_inc(pp_t, 1)

                            def p_values(r):
                                m = PTILES[r][1]
                                nk = (KW[r] + P - 1) // P
                                pe.wait_ge(pp_e, H * 5 + r + 1)
                                pe.wait_ge(op_e, H * 5 + r + 2)
                                apart(pe, started)
                                for kt in range(nk):
                                    k1 = min(P, KW[r] - P * kt)
                                    mm = pe.matmul(PB[:, 3, 0:m], VN[0:k1, kt, HD * n:HD * n + HD],
                                                   PPT[0:k1, m * kt:m * kt + m], start=(kt == 0), stop=(kt == nk - 1))
                                mm.then_inc(op_mm, 1)

                            pe.wait_ge(qst_done, H + 1)
                            p_logits(0)
                            gate(0)
                            for r in range(4):
                                p_logits(r + 1)
                                p_transposes(r)
                                gate(r + 1)
                                p_values(r)
                            p_transposes(4)
                            p_values(4)
                pe.wait_ge(op_e, l * 40 + 42)
                pe.wait_ge(cso_ready, l + 1)
                pe.transpose(PB[:, 0, 0:P], CSO[:, 0:16, :].rearrange("p r c -> p (r c)"), ident[:, :])
                pe.transpose(PB[0:16, 0, P:2 * P], CSO[:, 16:18, :].rearrange("p r c -> p (r c)"),
                             ident[:, :]).then_inc(cso_t, 1)
                apart(pe, started)
                with pe.Fori(0, 4) as i:
                    for s in range(2):
                        unit(s, l * USES[s] + i + phase_use(s, CONV), AHh, AHl, ready=l * 72 + 9 if s == 0 else None)

                pe.wait_ge(qp_ready, l + 1)
                pe.wait_ge(cso_e, l + 1)
                for s in range(2):
                    pe.wait_ge(evac_done[s], use(s, phase_use(s, 6)) + 1)
                banks = [PS[0][:, 0, :], PS[0][:, 1, :], PS[1][:, 0, :]]
                new_l = PS[1][:, 1, 0:RS]
                out_s = PS[1][:, 1, KV_W:2 * KV_W]
                for g in range(2):
                    def evacuated(t):
                        pe.wait_ge((kt_ea, kt_ed)[t % 2], l * 32 + 16 * g + t // 2 + 1)

                    def k_transposes(t):
                        q, b4 = t // 4, t % 4
                        c, n = q // KVH, q % KVH
                        if q in (0, 4):
                            pe.wait_ge(kv_in[q // 4][b4], l * 64 + 32 * g + 16)
                        if t >= 3:
                            evacuated(t - 3)
                        for j in range(4):
                            tr = pe.transpose(banks[t % 3][:, P * j:P * j + P],
                                              KVB[c // 2][b4][:, 4 * (c % 2) + j, HD * n:HD * n + HD], ident[:, :])
                        tr.then_inc(kt_t, 1)

                    for t in range(3):
                        k_transposes(t)
                    for q in range(8):
                        c, n = q // KVH, q % KVH
                        for t in range(4 * q + 3, min(4 * q + 7, 32)):
                            k_transposes(t)
                        evacuated(4 * q + 2)
                        evacuated(4 * q + 3)
                        for b4 in range(4):
                            mm = pe.matmul(PB[32 * b4:32 * b4 + 32, c, :],
                                           QP[:, 4 * g + b4, n].rearrange("p h s -> p (h s)"), KTR[b4][:, :],
                                           start=(n == 0), stop=False)
                        mm.then_inc(kt_mm, 1)
                        if n == KVH - 1:
                            if g == 0 and c == 0:
                                pe.wait_ge(masks_ready, l + 1)
                                apart(pe, started)
                            pe.matmul(PB[:, c, :], selb[:, g, :], MS[:, 512 * c:512 * c + 512], start=False,
                                      stop=True).then_inc(ls_mm, 1)
                        if q == 3:
                            if g == 1:
                                pe.wait_ge(ot_e, l * 2 + 1)
                                apart(pe, started)
                            for b4 in range(4):
                                for m in range(KVH):
                                    pe.matmul(new_l[32 * b4:32 * b4 + 32, :],
                                              QP[:, 4 * g + b4, m].rearrange("p h s -> p (h s)"),
                                              KT[:, m, RP:R], start=(m == 0), stop=False)
                            pe.matmul(new_l, selb[:, g, :], MS[:, PAST:KEYS_S], start=False, stop=True).then_inc(ls_mm, 1)

                    def pt_transposes(c):
                        w, kn = (4, P) if c < 4 else (1, RS)
                        pe.wait_ge(ls_exp, l * 10 + 5 * g + (c + 2 if c < 4 else 1))
                        if c >= 3:
                            pe.wait_ge(pt_e, l * 10 + 5 * g + c - 2)
                        for j in range(w):
                            tr = pe.transpose(banks[c % 3][0:kn, P * j:P * j + P],
                                              PS_S[:, 512 * c + P * j:512 * c + P * j + kn], ident[:, :])
                        tr.then_inc(pt_t, 1)

                    for c in range(3):
                        pt_transposes(c)
                    for c in range(5):
                        w, kn = (4, P) if c < 4 else (1, RS)
                        pe.wait_ge(pt_e, l * 10 + 5 * g + c + 1)
                        apart(pe, started)
                        for j in range(w):
                            for b4 in range(4):
                                if c in (0, 2) and j == 0:
                                    pe.wait_ge(kv_in[c // 2][b4], l * 64 + 32 * g + 32)
                                pt = KTR[c % 4][0:kn, P * j + 32 * b4:P * j + 32 * b4 + 32]
                                vv = KVB[c // 2][b4][:, 4 * (c % 2) + j, :] if c < 4 else VN[0:RS, 5, :]
                                mm = pe.matmul(out_s[32 * b4:32 * b4 + 32, :], pt, vv,
                                               start=(c == 0 and j == 0), stop=(c == 4))
                        mm.then_inc(pv_mm, 1)
                        if c + 3 < 5:
                            pt_transposes(c + 3)
                    pe.wait_ge(os_e, l * 2 + g + 1)
                    for n in range(KVH):
                        tr = pe.transpose(PS[1][:, 1, P * n:P * n + P], O_S[:, HD * n:HD * n + HD], ident[:, :])
                    tr.then_inc(ot_t, 1)

                apart(pe, started)
                with pe.Fori(0, 4) as i:
                    for s in range(2):
                        unit(s, l * USES[s] + i + phase_use(s, 6), AXh, AXl, ready=l * 72 + 17 if s == 0 else None)
                apart(pe, started)
                with pe.Fori(0, 4) as i:
                    for s in range(2):
                        unit(s, l * USES[s] + i + phase_use(s, 7), AHh, AHl, ready=l * 72 + 25 if s == 0 else None)

                def layer_norm(j):
                    for s in range(2):
                        pe.wait_ge(evac_done[s], use(s, phase_use(s, 8 + 8 * j)) + 1)
                    for h in range(2):
                        for c in range(KC):
                            mm = pe.matmul(PS[0][:, h, 0:RH], ones[:, :], X[:, c, RH * h:RH * h + RH],
                                           start=(c == 0), stop=(c == KC - 1))
                        mm.then_inc(ln_sum, 1)
                    for h in range(2):
                        pe.wait_ge(ln_sq, l * 4 + 2 * j + h + 1)
                        for c in range(KC):
                            mm = pe.matmul(PS[1][:, h, 0:RH], ones[:, :], SQ[:, c, RH * h:RH * h + RH],
                                           start=(c == 0), stop=(c == KC - 1))
                        mm.then_inc(ln_var, 1)

                layer_norm(0)
                pe.wait_ge(ln_sd, l * 4 + 2)
                apart(pe, started)
                with pe.Fori(0, NG) as g:
                    apart(pe, started)
                    with pe.Fori(0, 4) as i:
                        for s in range(2):
                            unit(s, l * USES[s] + g * 8 + i + phase_use(s, 8), AXh, AXl,
                                 ready=l * 72 + 33 if s == 0 else None)
                    apart(pe, started)
                    with pe.Fori(0, 4) as i:
                        for s in range(2):
                            unit(s, l * USES[s] + g * 8 + i + phase_use(s, 9), AHh, AHl,
                                 ready=l * 72 + g * 8 + 41 if s == 0 else None)
                layer_norm(1)
                pe.wait_ge(ln_sd, l * 4 + 4)

            pe.wait_ge(a_ready, DEPTH * 72 + 8)
            for t, (c0, n) in enumerate([(16 + P * j, P) for j in range(4)] + [(RP, RS)]):
                if t >= 2:
                    pe.wait_ge(y_e, t - 1)
                for c in range(KC):
                    tr = pe.transpose(PS[t % 2][0:n, c // 4, P * (c % 4):P * (c % 4) + P], X[:, c, c0:c0 + n], ident[:, :])
                tr.then_inc(y_t, 1)

        @block.scalar
        def _(act):
            def high(s, n):
                act.wait_ge(loaded[s], n * 16 + 16)
                act.wait_ge(mm_done[s], n + 1)
                act.copy(WH[s][:, :, :], ST[s][:, :, :]).then_inc(hi_done[s], 1)

            def halves(dst):
                return dst.rearrange("p (h r) -> p h r", h=2)

            def evac(s, n, fn):
                high(s, n + 1)
                act.wait_ge(mm_done[s], n + 2)
                apart(act, started)
                fn().then_inc(evac_done[s], 1)

            for s in range(2):
                high(s, 0)
            act.wait_ge(const_in, 16 * (NPG + 7 + 10))
            act.copy(identb[:, :], ident[:, :])
            act.mul(causb[:, :], caus[:, :], NEG_MASK)
            act.copy(selb[:, :, :], SELF[:, :, :])
            for t, (c0, n) in enumerate([(0, 16)] + [(16 + P * j, P) for j in range(4)] + [(RP, RS)]):
                act.wait_ge(setup_t, t + 1)
                for hb in range(2):
                    e = act.copy(X[:, 4 * hb:4 * hb + 4, c0:c0 + n],
                                 PS[t % 2][:, hb, :].rearrange("p (c r) -> p c r", r=P)[:, :, 0:n])
                e.then_inc(setup_e, 1)

            apart(act, started)
            with act.Fori(0, DEPTH) as l:
                def use(s, n):
                    return l * USES[s] + n

                act.wait_ge(a_ready, l * 72 + 8)
                for s, n, dst in ((0, 0, QI[:, 0, :]), (1, 0, QI[:, 1, :]), (0, 1, QI[:, 2, :]), (1, 1, QI[:, 3, :]),
                                  (0, 2, KI[:, :]), (0, 3, KT[:, 0, :]), (1, 2, KT[:, 1, :]),
                                  (0, 4, VT[:, 0, :]), (1, 3, VT[:, 1, :])):
                    evac(s, use(s, n), lambda: act.copy(halves(dst), PS[s][:, :, 0:RH]))
                apart(act, started)
                with act.Fori(0, 4) as i:
                    for s in range(2):
                        evac(s, l * USES[s] + i + phase_use(s, -1),
                             lambda: act.copy(halves(Q[:, bass.ds(i * 2 + s, 1), :].rearrange("p o r -> p (o r)")),
                                              PS[s][:, :, 0:RH]))
                act.wait_ge(ki_t, l + 1)
                act.copy(WKN[:, 0:4, :], PB[:, 0, 0:320].rearrange("p (t d) -> p t d", t=4)[:, :, 0:72])
                act.copy(WKN[0:16, 4, :], PB[0:16, 0, 320:392])
                act.copy(WKN[0:RS, 5, :], PB[0:RS, 0, 400:472]).then_inc(ki_e, 1)
                act.wait_ge(ki_e, l + 1)
                act.dma_start(a["o_ik"][bass.ds(l, 1), 0, 0:512, :].rearrange("o (t p) d -> (o p) t d", p=P),
                              WKN[:, 0:4, 0:ID]).then_inc(out_small, 16)
                act.dma_start(a["o_ik"][bass.ds(l, 1), 0, 512:RP, :].rearrange("o p d -> (o p) d"),
                              WKN[0:16, 4, 0:ID]).then_inc(out_small, 16)
                act.dma_start(a["o_iks"][bass.ds(l, 1)].rearrange("o b s d -> (o b s) d"),
                              WKN[0:RS, 5, 0:ID]).then_inc(out_small, 16)
                for t, (c0, n) in enumerate(TILES):
                    act.wait_ge(kv_t, l * 6 + t + 1)
                    if t >= 2:
                        act.wait_ge(out_k[t % 2], l * 48 + 16 * (t // 2))
                    act.copy(KNS[t % 2][0:n, :], PB[0:n, 2 + t % 2, 0:256])
                    act.copy(VN[0:n, t, :], PB[0:n, 2 + t % 2, 256:512]).then_inc(kv_e, 1)
                    act.wait_ge(kv_e, l * 6 + t + 1)
                    apart(act, started)
                    if t < 5:
                        kd = a["o_k"][bass.ds(l, 1), 0, c0:c0 + n].rearrange("o r h d -> (o r) (h d)")
                        vd = a["o_v"][bass.ds(l, 1), 0, c0:c0 + n].rearrange("o r h d -> (o r) (h d)")
                    else:
                        kd = a["o_ks"][bass.ds(l, 1)].rearrange("o b s h d -> (o b s) (h d)")
                        vd = a["o_vs"][bass.ds(l, 1)].rearrange("o b s h d -> (o b s) (h d)")
                    act.dma_start(kd, KNS[t % 2][0:n, :]).then_inc(out_k[t % 2], 16)
                    act.dma_start(vd, VN[0:n, t, :]).then_inc(out_v, 16)
                act.wait_ge(q_ready, l + 1)
                j = 0
                for r in range(1, 5):
                    n = PTILES[r][1]
                    for h in range(IH):
                        act.wait_ge(sc_mm, l * 32 + j + 1)
                        if j >= 2:
                            act.wait_ge(sc_acc, l * 32 + j - 1)
                        act.activation(RELU_P[j % 2][0:n, 0:KW[r]],
                                       PS[j % 2][0:n].rearrange("p b k -> p (b k)")[:, 0:KW[r]],
                                       ACT.Relu).then_inc(sc_relu, 1)
                        j += 1
                def relu_group(g):
                    act.wait_ge(ss_step, l * 4 + 2 * g + 2)
                    for par in range(2):
                        e = act.activation(RELU_S[g][:, 1024 * par:1024 * par + 1024],
                                           PS[par][:, :, :].rearrange("p j t -> p (j t)"), ACT.Relu)
                    e.then_inc(ss_relu, 1)

                for t in range(16):
                    act.wait_ge(kit_t, l * 16 + t + 1)
                    if t >= 4:
                        act.wait_ge(ss_step, l * 4 + t // 4)
                    act.copy(KIT[t % 4][:, :], PB[:, t % 4, :]).then_inc(kit_e, 1)
                    if t == 11:
                        relu_group(0)
                relu_group(1)
                act.wait_ge(ss_mm, l + 1)
                for g in range(2):
                    e = act.activation(RELU_S[g][:, PAST:KEYS_S], PB[:, 0, RS * g:RS * g + RS], ACT.Relu)
                e.then_inc(ss_relu, 1)

                act.wait_ge(ue_init, l + 1)
                act.wait_ge(out_k[0], l * 48 + 48)
                act.wait_ge(out_k[1], l * 48 + 48)
                act.wait_ge(mp_ready, l + 1)
                apart(act, started)
                with act.Fori(0, KC // 2) as pair:
                    for hb in range(2):
                        c = pair * 2 + hb
                        H = l * HEADS + c

                        def gate_n(k):
                            k += 5 * hb
                            return k % 2, l * USES[k % 2] + pair * 5 + gate_use(k % 2, k)

                        def high_only(k):
                            s, n = gate_n(k)
                            high(s, n + 1)

                        def h_rows():
                            if hb == 1:
                                s, n = 0, l * USES[0] + pair * 5 + gate_use(0, 2)
                            else:
                                s, n = 1, l * USES[1] + pair * 5 + gate_use(1, 7) - 5
                            act.wait_ge(evac_done[s], n + 2)
                            s = gate_n(0)[0]
                            act.copy(UE[:, 2:2 + RH], PS[s][:, 0, 0:RH])
                            act.copy(UE[:, 2 + RH:2 + RP], PS[s][:, 1, 0:RP - RH])
                            return act.copy(UE[:, 2 + RP:UE_W].rearrange("p (b t) -> p b t", t=6)[:, :, 2:6],
                                            PS[s][:, 1, RP - RH:RH].rearrange("p (b t) -> p b t", t=NS))

                        def minus_exp(k, dst):
                            s, n = gate_n(k)
                            evac(s, n, lambda: act.activation(halves(dst[:, bass.ds(c, 1), :].rearrange("p o r -> p (o r)")),
                                                              PS[s][:, :, 0:RH], ACT.Exp, scale=-1.0))

                        def p_exp(r):
                            m = PTILES[r][1]
                            act.wait_ge(lp_max, H * 5 + r + 1)
                            act.wait_ge(pp_t, H * 5 + r + (2 if r == 0 else 1))
                            act.activation(PP[r % 2][0:m, 0:KW[r]],
                                           PB[0:m].rearrange("p b k -> p (b k)")[:, 512 * (r % 2):512 * (r % 2) + KW[r]],
                                           ACT.Exp, bias=stp[0:m, r % 2, 0:1], scale=SC_HD,
                                           accum_out=stp[0:m, r % 2, 1:2]).then_inc(lp_exp, 1)

                        def p_out(r):
                            c0, m = PTILES[r]
                            act.wait_ge(op_mm, H * 5 + r + 3)
                            apart(act, started)
                            act.copy(Q[:, bass.ds(c, 1), c0:c0 + m].rearrange("p o r -> p (o r)"),
                                     PB[:, 3, 0:m]).then_inc(op_e, 1)

                        apart(act, started)
                        act.copy(QST[:, :], Q[:, bass.ds(c, 1), 0:RP].rearrange("p o r -> p (o r)")).then_inc(qst_done, 1)
                        p_exp(0)
                        s, n = gate_n(0)
                        evac(s, n, h_rows)
                        p_exp(1)
                        high_only(1)
                        p_out(0)
                        p_exp(2)
                        high_only(2)
                        p_out(1)
                        p_exp(3)
                        minus_exp(3, SG)
                        p_out(2)
                        p_exp(4)
                        minus_exp(4, BB)
                        p_out(3)
                        p_out(4)
                act.wait_ge(cso_t, l + 1)
                act.wait_ge(out_small, l * 48 + 48)
                act.copy(CSN[:, 0, :], PB[:, 0, 0:P])
                act.copy(CSN[0:16, 1, :], PB[0:16, 0, P:2 * P]).then_inc(cso_e, 1)
                act.wait_ge(cso_e, l + 1)
                act.dma_start(a["o_cs"][bass.ds(l, 1)].rearrange("o b t (c d) -> (o b t c) d", d=P),
                              CSN[:, 0, :]).then_inc(out_c, 16)
                act.dma_start(a["o_c"][bass.ds(l, 1), 0].rearrange("o t (c d) -> (o t c) d", d=P),
                              CSN[0:16, 1, :]).then_inc(out_c, 16)
                apart(act, started)
                with act.Fori(0, 4) as i:
                    for s in range(2):
                        high(s, l * USES[s] + i + (phase_use(s, CONV) + 1))

                banks = [PS[0][:, 0, :], PS[0][:, 1, :], PS[1][:, 0, :]]
                act.wait_ge(qp_ready, l + 1)
                for g in range(2):
                    for t in range(0, 32, 2):
                        act.wait_ge(kt_t, l * 64 + 32 * g + t + 1)
                        if t >= 4:
                            act.wait_ge(kt_mm, l * 16 + 8 * g + t // 4)
                        act.copy(KTR[t % 4][:, :], banks[t % 3]).then_inc(kt_ea, 1)
                    act.wait_ge(ls_max, l * 2 + g + 1)
                    for c in (4, 0, 1, 2, 3):
                        src, w = (PB[:, c, :], 512) if c < 4 else (PS[1][:, 1, 0:RS], RS)
                        act.activation(PS_S[:, 512 * c:512 * c + w], src, ACT.Exp, bias=st[:, 5:6], scale=SC_HD,
                                       accum_out=st[:, 6 + c:7 + c]).then_inc(ls_exp, 1)
                    act.wait_ge(ot_t, l * 2 + g + 1)
                    for n in range(KVH):
                        col = RP + NS * 4 * g
                        e = act.copy(Q[:, GRP * n:GRP * n + GRP, col:col + 4 * NS].rearrange("p h (b s) -> p b h s", s=NS),
                                     PS[1][:, 1, P * n:P * n + P].rearrange("p (b h s) -> p b h s", b=4, s=NS)
                                     [:, :, GRP * n:GRP * n + GRP, :])
                    e.then_inc(ot_e, 1)

                for ph in (6, 7):
                    apart(act, started)
                    with act.Fori(0, 4) as i:
                        for s in range(2):
                            high(s, l * USES[s] + i + (phase_use(s, ph) + 1))

                def layer_norm(j):
                    for h in range(2):
                        act.wait_ge(ln_dev, l * 4 + 2 * j + h + 1)
                        act.activation(SQ[:, :, RH * h:RH * h + RH], X[:, :, RH * h:RH * h + RH], ACT.Square).then_inc(ln_sq, 1)
                    for h in range(2):
                        act.wait_ge(ln_var, l * 4 + 2 * j + h + 1)
                        act.activation(SD[:, RH * h:RH * h + RH], PS[1][:, h, 0:RH], ACT.Sqrt, bias=eps[:, 0:1]).then_inc(ln_sd, 1)
                    for c in range(KC):
                        if c == 0:
                            act.wait_ge(ln_norm, l * 4 + 2 * j + 2)
                        act.activation(X[:, c, :], X[:, c, :], ACT.Identity, bias=PL[:, 16 * j + 8 + c:16 * j + 9 + c],
                                       scale=PL[:, 16 * j + c:16 * j + c + 1]).then_inc(ln_aff, 1)

                layer_norm(0)
                apart(act, started)
                with act.Fori(0, NG) as g:
                    apart(act, started)
                    with act.Fori(0, 4) as i:
                        for s in range(2):
                            n = l * USES[s] + g * 8 + i + phase_use(s, 8)
                            high(s, n + 1)
                            act.wait_ge(mm_done[s], n + 2)
                            act.wait_ge(a_ready, l * 72 + g * 8 + i * 2 + s + 39)
                            act.activation(halves(MT[s][:, :]), PS[s][:, :, 0:RH], ACT.Relu).then_inc(relu_h, 1)
                    apart(act, started)
                    with act.Fori(0, 4) as i:
                        for s in range(2):
                            high(s, l * USES[s] + g * 8 + i + (phase_use(s, 9) + 1))
                layer_norm(1)
                act.wait_ge(out_small, l * 48 + 48)
                act.wait_ge(out_v, l * 96 + 96)
                act.wait_ge(out_c, l * 32 + 32)

            for t, (c0, n) in enumerate([(16 + P * j, P) for j in range(4)] + [(RP, RS)]):
                act.wait_ge(y_t, t + 1)
                if t >= 2:
                    act.wait_ge(out_y[t % 2], 16 * (t // 2))
                act.copy(NAT[t % 2][0:n, :], PS[t % 2][0:n].rearrange("p b k -> p (b k)")).then_inc(y_e, 1)
                act.wait_ge(y_e, t + 1)
                dst = a["o_y"][0, P * t:P * t + P, :] if t < 4 else a["o_ys"].rearrange("b s d -> (b s) d")
                act.dma_start(dst, NAT[t % 2][0:n, :]).then_inc(out_y[t % 2], 16)
            act.wait_ge(out_y[0], 16 * 3)
            act.wait_ge(out_y[1], 16 * 2)
            for i in range(2):
                act.wait_ge(out_k[i], DEPTH * 48)

        def apart_drain(eng):
            apart(eng, started)
            return eng.drain()

        @block.vector
        def _(dve):
            own = Chain(dve, dve_own, started)

            for s in range(2):
                dve.sem_inc(evac_done[s], 1)
            for q in (lp_exp, pp_t, op_mm, op_e):
                dve.sem_inc(q, 2)
            dve.memset(ones[:, :], 1.0 / DM)
            dve.memset(eps[:, :], EPS)
            dve.wait_ge(const_in, 16 * (NPG + 7 + 10))
            def half_rows():
                for h in range(2):
                    e = dve.tensor_scalar(IDXH[:, h, :], IDX[:, :], 2.0, float(h), ALU.mult, ALU.add)
                return e

            own.link(dve.tensor_scalar(IDX[:, :], PTB[:, :], float(PAGE // TPP), SEG[:, 0:1], ALU.mult, ALU.add))
            half_rows().then_inc(idx_ready, 1)
            dve.wait_ge(params_t, 1)
            own.link(dve.tensor_copy(PTT[:, :], PB[:, 0, 0:112]))
            dve.wait_ge(setup_e, 6)

            def split(hi, lo, src):
                own.link(dve.tensor_copy(hi, src))
                dve.tensor_tensor(lo, src, hi.bitcast(F32), ALU.subtract).then_inc(a_ready, 1)

            def chunk(t, c):
                return t[:, bass.ds(c, 1), :].rearrange("p o r -> p (o r)")

            def halves(v):
                return v.rearrange("p (h r) -> p h r", h=2)

            with own.fori(KC, 1) as c:
                split(chunk(AXh, c), chunk(AXl, c), chunk(X, c))

            with own.fori(DEPTH, LAYER_LINKS) as l:
                def use(s, n):
                    return l * USES[s] + n

                def rope(v, cos, sin, mask, tmp):
                    apart(dve, started)
                    own.link(dve.stream_shuffle(tmp, v, mask))
                    dve.tensor_tensor(v, v, cos, ALU.mult)
                    own.link(dve.tensor_tensor(tmp, tmp, sin, ALU.mult))
                    own.link(dve.tensor_tensor(v, v, tmp, ALU.add))

                own.link(dve.tensor_copy(PL[:, :], PTT[:, bass.ds(l * 56, 56)]))
                dve.wait_ge(tables_in, l * 64 + 64)
                for c in range(4):
                    dve.wait_ge(evac_done[c % 2], use(c % 2, c // 2) + 2)
                    rope(QI[:, c, :], ICOS[:, :], ISIN[:, :], rope_swap(IDX_ROT // 2), ROPE[:, :])
                for hp in range(2):
                    for par in range(2):
                        e = dve.tensor_copy(QS[ID * hp:ID * hp + ID, :, par::2, :],
                                            QI[ID * par:ID * par + ID, :, RP:R].rearrange("p c (b s) -> p b c s", s=NS))
                e.then_inc(qi_roped, 1)
                dve.wait_ge(evac_done[0], use(0, 2) + 2)
                rope(KI[0:ID, :], ICOS[0:ID, :], ISIN[0:ID, :], rope_swap(IDX_ROT // 2), ROPE[0:ID, :])
                dve.tensor_copy(KD[0:ID, :], KI[0:ID, :])
                dve.tensor_copy(KD[ID:P, :], KI[0:ID, :]).then_inc(ki_ready, 1)
                for h in range(KVH):
                    dve.wait_ge(evac_done[h], use(h, 3 - h) + 2)
                    rope(KT[0:32, h, :], QCOS[:, :], QSIN[:, :], rope_swap(ROT // 2), ROPE[0:32, :])
                apart_drain(dve).then_inc(kv_ready, 1)
                dve.wait_ge(ki_e, l + 1)
                dve.tensor_scalar(WKN[:, 1:4, ID:ID + IH], WKN[:, 1:4, ID:ID + IH], SC_WI, None, ALU.mult)
                own.link(dve.tensor_scalar(WKN[0:16, 4, ID:ID + IH], WKN[0:16, 4, ID:ID + IH], SC_WI, None, ALU.mult))
                dve.wait_ge(wi_mm, l + 1)
                dve.tensor_copy(SCT[:, :], PB[:, 1, P:2 * P])
                for g in range(2):
                    e = dve.scalar_tensor_tensor(WIB[:, g, :], PB[:, 1, 0:RS], SC_WI, pick[:, g, :], ALU.mult, ALU.mult)
                e.then_inc(wib_ready, 1)
                for c in range(KC):
                    s = c % 2
                    dve.wait_ge(evac_done[s], use(s, phase_use(s, -1) + c // 2 + 2))
                    rope(Q[0:32, c, :], QCOS[:, :], QSIN[:, :], rope_swap(ROT // 2), ROPE[0:32, :])
                apart_drain(dve).then_inc(q_ready, 1)

                j = 0
                for r in range(1, 5):
                    c0, n = PTILES[r]
                    for h in range(IH):
                        dve.wait_ge(sc_relu, l * 32 + j + 1)
                        if j > 0:
                            dve.wait_ge(sc_acc, l * 32 + j)
                        w = WKN[0:n, r, ID + h:ID + h + 1]
                        if h == 0:
                            e = dve.tensor_scalar(TK[r][0:n, :], RELU_P[j % 2][0:n, 0:KW[r]], w, None, ALU.mult)
                        else:
                            e = dve.scalar_tensor_tensor(TK[r][0:n, :], RELU_P[j % 2][0:n, 0:KW[r]], w, TK[r][0:n, :],
                                                         ALU.mult, ALU.add)
                        e.then_inc(sc_acc, 1)
                        j += 1
                dve.wait_ge(sc_acc, l * 32 + 32)

                def take_eight(rows):
                    for i, (tk, n) in enumerate(rows):
                        e = dve.max(top[0:n, i, :], tk)
                    own.link(e, alone=True)
                    for i, (tk, n) in enumerate(rows):
                        e = dve.match_replace(tk, top[0:n, i, :], tk, NEG_TAKEN)
                    own.link(e, alone=True)

                for r in range(1, 5):
                    n = PTILES[r][1]
                    e = dve.scalar_tensor_tensor(TK[r][0:n, P * r:P * r + n], caus[0:n, 0:n], NEG_KEY,
                                                 TK[r][0:n, P * r:P * r + n], ALU.mult, ALU.add)
                own.link(e)
                with own.fori(TOPK_P // 8, 2):
                    take_eight([(TK[r][0:PTILES[r][1], :], PTILES[r][1]) for r in range(1, 5)])
                dve.wait_ge(kv_e, l * 6 + 6)
                for r in range(1, 5):
                    n = PTILES[r][1]
                    e = dve.tensor_scalar(MP[r][0:n, :], TK[r][0:n, :], NEG_CUT, NEG_MASK, ALU.is_gt, ALU.mult)
                e.then_inc(mp_ready, 1)
                dve.wait_ge(w_mm, l + 1)
                past = TKS[:, 0:PAST].rearrange("r (p j a) -> r a j p", j=KC, a=2)
                for par in range(2):
                    for jh in range(2):
                        dve.tensor_copy(past[:, par, 4 * jh:4 * jh + 4, :],
                                        PS[par][0:RS, jh, :].rearrange("r (j p) -> r j p", j=4))
                dve.scalar_tensor_tensor(TKS[:, PAST:KEYS_S], newok[:, :], NEG_KEY, PB[0:RS, 1, 0:RS],
                                         ALU.mult, ALU.add).then_inc(tks_ready, 1)
                dve.wait_ge(tks_ready, l + 1)
                dve.memset(UE[:, 0:2], 0.0).then_inc(ue_init, 1)
                past_t = UE[:, 2 + RP:UE_W].rearrange("p (b t) -> p b t", t=6)
                state = SCT[:, :].rearrange("p (b t c) -> p b t c", b=NB, c=KC)

                with own.fori(KC // 2, PAIR_LINKS) as pair:
                    for hb in range(2):
                        c = pair * 2 + hb
                        H = l * HEADS + c

                        def gate_n(k):
                            k += 5 * hb
                            return k % 2, l * USES[k % 2] + pair * 5 + gate_use(k % 2, k)

                        def p_max(r):
                            m = PTILES[r][1]
                            dve.wait_ge(lp_mm, H * 5 + r + 1)
                            dve.wait_ge(lp_exp, H * 5 + r + (2 if r == 0 else 1))
                            own.link(dve.tensor_reduce(
                                stp[0:m, r % 2, 2:3],
                                PB[0:m].rearrange("p b k -> p (b k)")[:, 512 * (r % 2):512 * (r % 2) + KW[r]],
                                AX_X, ALU.max))
                            dve.tensor_scalar(stp[0:m, r % 2, 0:1], stp[0:m, r % 2, 2:3], -SC_HD, None, ALU.mult
                                              ).then_inc(lp_max, 1)

                        def p_norm(r):
                            m = PTILES[r][1]
                            dve.wait_ge(lp_exp, H * 5 + r + 3)
                            own.link(dve.reciprocal(stp[0:m, r % 2, 3:4], stp[0:m, r % 2, 1:2]))
                            dve.tensor_scalar(PP[r % 2][0:m, 0:KW[r]], PP[r % 2][0:m, 0:KW[r]], stp[0:m, r % 2, 3:4],
                                              None, ALU.mult).then_inc(pp_norm, 1)

                        def p_turned(r):
                            m = PTILES[r][1]
                            full = (KW[r] // P) * m
                            dve.wait_ge(pp_t, H * 5 + r + 3)
                            dve.wait_ge(op_mm, H * 5 + r + 2)
                            if KW[r] % P:
                                dve.tensor_copy(PPT[0:KW[r] % P, full:full + m], PB[0:KW[r] % P, 2, full:full + m])
                            dve.tensor_copy(PPT[:, 0:full], PB[:, 2, 0:full]).then_inc(pp_e, 1)

                        def gate_c():
                            s, n = gate_n(1)
                            dve.wait_ge(evac_done[gate_n(0)[0]], gate_n(0)[1] + 2)
                            dve.wait_ge(mm_done[s], n + 2)
                            for u, z in ((UE[:, 2:2 + RH], PS[s][:, 0, 0:RH]),
                                         (UE[:, 2 + RH:2 + RP], PS[s][:, 1, 0:RP - RH]),
                                         (past_t[:, :, 2:6], PS[s][:, 1, RP - RH:RH].rearrange("p (b t) -> p b t", t=NS))):
                                e = dve.tensor_tensor(u, z, u, ALU.mult)
                            e.then_inc(evac_done[s], 1)
                            dve.wait_ge(evac_done[s], n + 2)
                            dve.tensor_copy(CSO[:, 16:18, bass.ds(c, 1)].rearrange("p t o -> p (t o)"), UE[:, RP:RP + 2])
                            dve.tensor_copy(CSO[:, 0:16, bass.ds(c, 1)].rearrange("p (b t) o -> p b (t o)", t=2),
                                            past_t[:, :, 4:6])

                        def short_conv():
                            w = [PL[:, bass.ds(c + (32 + KC * t), 1)] for t in range(CW)]
                            cys = CY[:, RP:R].rearrange("p (b t) -> p b t", t=NS)
                            dve.tensor_scalar(CY[:, 0:RP], UE[:, 0:RP], w[0], None, ALU.mult)
                            own.link(dve.tensor_scalar(cys, past_t[:, :, 0:NS], w[0], None, ALU.mult))
                            for t in range(1, CW):
                                dve.scalar_tensor_tensor(CY[:, 0:RP], UE[:, t:t + RP], w[t], CY[:, 0:RP], ALU.mult, ALU.add)
                                own.link(dve.scalar_tensor_tensor(cys, past_t[:, :, t:t + NS], w[t], cys, ALU.mult, ALU.add))

                        def gate_b():
                            s, n = gate_n(2)
                            dve.wait_ge(mm_done[s], n + 2)
                            dve.tensor_tensor(halves(CY[:, :]), PS[s][:, :, 0:RH], halves(CY[:, :]), ALU.mult
                                              ).then_inc(evac_done[s], 1)
                            dve.wait_ge(evac_done[s], n + 2)
                            split(chunk(AHh, c), chunk(AHl, c), CY[:, :])

                        own.link(dve.tensor_copy(past_t[:, :, 0:2],
                                                 state[:, :, :, bass.ds(c, 1)].rearrange("p b t o -> p b (t o)")))
                        p_max(0)
                        take_eight([(TKS[:, :], RS)])
                        p_norm(0)
                        p_max(1)
                        p_turned(0)
                        p_norm(1)
                        gate_c()
                        short_conv()
                        p_max(2)
                        p_turned(1)
                        p_norm(2)
                        gate_b()
                        take_eight([(TKS[:, :], RS)])
                        p_max(3)
                        p_turned(2)
                        p_norm(3)
                        take_eight([(TKS[:, :], RS)])
                        p_max(4)
                        p_turned(3)
                        p_norm(4)
                        take_eight([(TKS[:, :], RS)])
                        p_turned(4)
                apart_drain(dve).then_inc(cso_ready, 1)
                own.link(dve.memset(QP[:, :, :, :, :], 0.0))
                for n in range(KVH):
                    e = dve.tensor_copy(QP[:, :, n, GRP * n:GRP * n + GRP, :],
                                        Q[:, GRP * n:GRP * n + GRP, RP:R].rearrange("p h (b s) -> p b h s", s=NS))
                e.then_inc(qp_ready, 1)

                def sigmoid(v):
                    own.link(dve.tensor_scalar(v, v, 1.0, None, ALU.add), alone=True)
                    own.link(dve.reciprocal(v, v))

                for s in range(2):
                    dve.wait_ge(evac_done[s], use(s, phase_use(s, CONV) + 1))
                with own.fori(4, 4) as i:
                    for s in range(2):
                        sigmoid(chunk(BB, i * 2 + s))
                        n = l * USES[s] + i + phase_use(s, CONV)
                        dve.wait_ge(mm_done[s], n + 2)
                        bb = halves(chunk(BB, i * 2 + s))
                        dve.tensor_tensor(bb, PS[s][:, :, 0:RH], bb, ALU.mult).then_inc(evac_done[s], 1)
                dve.tensor_scalar(MS[:, 0:PAST].rearrange("r (i p) -> r i p", p=P),
                                  TKS[:, 0:PAST].rearrange("r (p i) -> r i p", p=P), NEG_CUT, NEG_MASK,
                                  ALU.is_gt, ALU.mult)
                dve.tensor_scalar(MS[:, PAST:KEYS_S], TKS[:, PAST:KEYS_S], NEG_CUT, NEG_MASK,
                                  ALU.is_gt, ALU.mult).then_inc(masks_ready, 1)

                banks = [PS[0][:, 0, :], PS[0][:, 1, :], PS[1][:, 0, :]]

                def split_heads(c0, c1):
                    with own.fori(c1 - c0, 1) as c:
                        hi, lo, q = (chunk(t, c + c0)[:, 0:RP] for t in (AXh, AXl, Q))
                        own.link(dve.tensor_copy(hi, q))
                        dve.tensor_tensor(lo, q, hi.bitcast(F32), ALU.subtract)

                for g in range(2):
                    for t in range(1, 32, 2):
                        dve.wait_ge(kt_t, l * 64 + 32 * g + t + 1)
                        if t >= 4:
                            dve.wait_ge(kt_mm, l * 16 + 8 * g + t // 4)
                        dve.tensor_copy(KTR[t % 4][:, :], banks[t % 3]).then_inc(kt_ed, 1)
                        if t in (11, 19, 27):
                            c = (t - 11) // 8
                            dve.wait_ge(ls_mm, l * 10 + 5 * g + (c if c < 2 else 3) + 1)
                            dve.reduce_max(st[:, c:c + 1], PB[:, c, :], AX_X)
                            if c == 2:
                                dve.reduce_max(st[:, 4:5], PS[1][:, 1, 0:RS], AX_X)
                    dve.wait_ge(ls_mm, l * 10 + 5 * g + 5)
                    own.link(dve.reduce_max(st[:, 3:4], PB[:, 3, :], AX_X))
                    own.link(dve.reduce_max(st[:, 13:14], st[:, 0:5], AX_X))
                    dve.tensor_scalar(st[:, 5:6], st[:, 13:14], -SC_HD, None, ALU.mult).then_inc(ls_max, 1)
                    for c in range(5):
                        dve.wait_ge(pt_t, l * 10 + 5 * g + c + 1)
                        if c == 4:
                            dve.wait_ge(pv_mm, l * 10 + 5 * g + 1)
                        w, kn = (512, P) if c < 4 else (P, RS)
                        dve.tensor_copy(KTR[c % 4][0:kn, 0:w], banks[c % 3][0:kn, 0:w]).then_inc(pt_e, 1)
                    dve.wait_ge(ls_exp, l * 10 + 5 * g + 5)
                    own.link(dve.reduce_sum(st[:, 11:12], st[:, 6:11], AX_X))
                    own.link(dve.reciprocal(st[:, 12:13], st[:, 11:12]))
                    if g == 1:
                        dve.wait_ge(pv_mm, l * 10 + 7)
                        split_heads(0, 3)
                    dve.wait_ge(pv_mm, l * 10 + 5 * g + 5)
                    dve.tensor_scalar(O_S[:, :], PS[1][:, 1, KV_W:2 * KV_W], st[:, 12:13], None, ALU.mult
                                      ).then_inc(os_e, 1)
                split_heads(3, KC)
                dve.wait_ge(ot_e, l * 2 + 2)
                own.link(dve.tensor_copy(AXh[:, :, RP:R], Q[:, :, RP:R]))
                dve.tensor_tensor(AXl[:, :, RP:R], Q[:, :, RP:R], AXh[:, :, RP:R].bitcast(F32), ALU.subtract
                                  ).then_inc(a_ready, KC)
                with own.fori(4, 2 * 4) as i:
                    for s in range(2):
                        sigmoid(chunk(SG, i * 2 + s))
                        n = l * USES[s] + i + phase_use(s, 6)
                        dve.wait_ge(mm_done[s], n + 2)
                        dve.tensor_tensor(halves(MT[s][:, :]), PS[s][:, :, 0:RH], halves(chunk(SG, i * 2 + s)), ALU.mult
                                          ).then_inc(evac_done[s], 1)
                        dve.wait_ge(evac_done[s], n + 2)
                        own.link(dve.tensor_tensor(MT[s][:, :], MT[s][:, :], chunk(BB, i * 2 + s), ALU.add))
                        split(chunk(AHh, i * 2 + s), chunk(AHl, i * 2 + s), MT[s][:, :])
                apart(dve, started)
                with dve.Fori(0, 4) as i:
                    for s in range(2):
                        n = l * USES[s] + i + phase_use(s, 7)
                        dve.wait_ge(mm_done[s], n + 2)
                        x = halves(chunk(X, i * 2 + s))
                        dve.scalar_tensor_tensor(x, x, ALPHA, PS[s][:, :, 0:RH], ALU.mult, ALU.add
                                                 ).then_inc(evac_done[s], 1)

                def layer_norm(j):
                    for s in range(2):
                        dve.wait_ge(evac_done[s], use(s, phase_use(s, 8 + 8 * j) + 1))
                    for h in range(2):
                        dve.wait_ge(ln_sum, l * 4 + 2 * j + h + 1)
                        x = X[:, :, RH * h:RH * h + RH]
                        dve.tensor_tensor(x, x, PS[0][:, h, 0:RH].unsqueeze(1).to_broadcast([P, KC, RH]), ALU.subtract
                                          ).then_inc(ln_dev, 1)
                    for h in range(2):
                        dve.wait_ge(ln_sd, l * 4 + 2 * j + h + 1)
                        x = X[:, :, RH * h:RH * h + RH]
                        rs = RSTD[:, RH * h:RH * h + RH]
                        own.link(dve.reciprocal(rs, SD[:, RH * h:RH * h + RH]))
                        dve.tensor_tensor(x, x, rs.unsqueeze(1).to_broadcast([P, KC, RH]), ALU.mult).then_inc(ln_norm, 1)
                    for c in range(KC):
                        dve.wait_ge(ln_aff, l * 16 + 8 * j + c + 1)
                        split(AXh[:, c, :], AXl[:, c, :], X[:, c, :])

                layer_norm(0)
                dve.wait_ge(a_ready, l * 72 + 40)
                own.link(dve.tensor_scalar(X[:, :, :].rearrange("p c r -> p (c r)"), X[:, :, :].rearrange("p c r -> p (c r)"),
                                           ALPHA, None, ALU.mult))
                with own.fori(NG, 4 * 2 * 1) as g:
                    with own.fori(4, 2 * 1) as i:
                        for s in range(2):
                            n = l * USES[s] + g * 8 + i + phase_use(s, 8)
                            dve.wait_ge(relu_h, l * 32 + g * 8 + i * 2 + s + 1)
                            dve.scalar_tensor_tensor(halves(MT[2 + s][:, :]), PS[s][:, :, 0:RH], 0.0, halves(MT[s][:, :]),
                                                     ALU.max, ALU.mult).then_inc(evac_done[s], 1)
                            dve.wait_ge(evac_done[s], n + 2)
                            split(chunk(AHh, i * 2 + s), chunk(AHl, i * 2 + s), MT[2 + s][:, :])
                    apart(dve, started)
                    with dve.Fori(0, 4) as i:
                        for s in range(2):
                            n = l * USES[s] + g * 8 + i + phase_use(s, 9)
                            dve.wait_ge(mm_done[s], n + 2)
                            dve.wait_ge(evac_done[s], n + 1)
                            x = halves(chunk(X, i * 2 + s))
                            dve.tensor_tensor(x, x, PS[s][:, :, 0:RH], ALU.add).then_inc(evac_done[s], 1)
                own.link(dve.tensor_scalar(IDX[:, :], IDX[:, :], float(n_rows), None, ALU.add))
                half_rows().then_inc(idx_ready, 1)
                layer_norm(1)


def constants():
    import numpy as np

    f = np.float32
    pos = np.concatenate([np.arange(RP), np.tile(PAST + np.arange(NS), NB)]).astype(f)

    def table(rot, width):
        half = rot // 2
        inv = (f(500000.0) ** (-np.arange(half, dtype=f) * f(2.0) / f(rot))).astype(f)
        ang = (pos[None, :] * inv[:, None]).astype(f)
        cos, sin = np.ones((width, R), f), np.zeros((width, R), f)
        cos[:half] = cos[half:rot] = np.cos(ang)
        sin[:half], sin[half:rot] = -np.sin(ang), np.sin(ang)
        return cos, sin

    icos, isin = table(IDX_ROT, ID)
    qcos, qsin = table(ROT, 32)
    q = np.arange(P)
    sel = np.zeros((RS, 2, P), f)
    pick = np.zeros((P, 2, RS), f)
    for b in range(NB):
        for h in range(HEADS):
            for s in range(NS):
                row = 32 * (b % 4) + NS * h + s
                sel[NS * b + s, b // 4, row] = 1
                pick[row, b // 4, NS * b + s] = 1
    expand = np.zeros((P, P), f)
    for h in range(IH):
        expand[ID + h] = (q % 32) // NS == h
    r = np.arange(RS)
    newok = ~((r[:, None] // NS == r[None, :] // NS) & (r[None, :] <= r[:, None]))
    return {
        "c_ident": np.eye(P, dtype=f), "c_caus": (q[None, :] > q[:, None]).astype(f), "c_expand": expand,
        "c_pick": pick, "c_newok": newok.astype(f), "c_seg": (q % (PAGE // TPP)).astype(f)[:, None], "c_sel": sel,
        "c_icos": np.concatenate([icos, icos]), "c_isin": np.concatenate([isin, isin]), "c_qcos": qcos, "c_qsin": qsin,
    }


_INS = ["x_prompt", "x_sample", "cache_k", "cache_v", "cache_idx_k", "state_conv", "page_table", "meta_tokens",
        "w_in", "conv_w", "w_attn_out", "w_conv_out", "w_o", "ln1_g", "ln1_b", "w_up", "w_down", "ln2_g", "ln2_b"]
_OUTS = [("o_y", (1, SEQ, DM)), ("o_ys", (NB, NS, DM)), ("o_k", (DEPTH, 1, RP, KVH, HD)), ("o_v", (DEPTH, 1, RP, KVH, HD)),
         ("o_ik", (DEPTH, 1, RP, ID)), ("o_c", (DEPTH, 1, CW - 1, DM)), ("o_ks", (DEPTH, NB, NS, KVH, HD)),
         ("o_vs", (DEPTH, NB, NS, KVH, HD)), ("o_iks", (DEPTH, NB, NS, ID)), ("o_cs", (DEPTH, NB, CW - 1, DM))]


def kernel(**inputs):
    import numpy as _np
    import concourse.bacc as _bacc
    from concourse import mybir as _mybir
    from concourse.bass_utils import run_bass_kernel_spmd as _run

    nc = _bacc.Bacc("TRN2", target_bir_lowering=False, num_devices=1)
    arrays, aps = {}, {}
    data = {n: _np.ascontiguousarray(inputs[n]) for n in _INS}
    data.update(constants())
    for name, v in data.items():
        arrays[f"in_{name}_dram"] = v
        aps[name] = nc.dram_tensor(f"in_{name}_dram", v.shape, _mybir.dt.from_np(v.dtype), kind="ExternalInput").ap()
    for name, shape in _OUTS:
        aps[name] = nc.dram_tensor(f"{name}_dram", shape, F32, kind="ExternalOutput").ap()
    trunk_program(nc, aps)
    r = _run(nc, [arrays], core_ids=[0])
    return tuple(r.results[0][f"{name}_dram"] for name, _ in _OUTS)
```

```python
from contextlib import ExitStack, contextmanager

import concourse.bass as bass
from concourse import mybir

F32 = mybir.dt.float32
F32R = mybir.dt.float32r
BF16 = mybir.dt.bfloat16
I32 = mybir.dt.int32
U32 = mybir.dt.uint32
ACT = mybir.ActivationFunctionType
ALU = mybir.AluOpType
AX_X = mybir.AxisListType.X

P = 128
DM = 1024
KC = DM // P
DEPTH = 2
SEQ, N_META = 512, 16
RP = SEQ + N_META
NB, NS = 8, 4
RS = NB * NS
R = RP + RS
RH = R // 2
HEADS, KVH, HD = 8, 2, 128
GRP = HEADS // KVH
IH, ID = 8, 64
ROT, IDX_ROT = HD // 4, ID // 4
LAYER_LINKS, HEAD_LINKS = 458, 16
KV_W = KVH * HD
PAST, PAGE = 2048, 128
NPG = PAST // PAGE
TPP = PAST // P
KEYS_S = PAST + RS
TOPK_P, TOPK_S = SEQ // 4, 256
CW = 3
DFF = 4096
NG = DFF // DM
P_TOTAL = 7240
COL_Q, COL_K, COL_V, COL_QI, COL_KI = 0, 1024, 1280, 1536, 2048
COL_H, COL_BG, COL_CG, COL_GA, COL_GB = 2120, 3144, 4168, 5192, 6216
UE_W = 2 + RP + NB * (2 + NS)
ALPHA = float((2 * DEPTH) ** 0.25)
EPS = 1e-5
SC_HD = float(HD) ** -0.5
SC_WI = float(IH) ** -0.5 * float(ID) ** -0.5
NEG_KEY = -3.0e38
NEG_TAKEN = -3.3e38
NEG_CUT = -3.2e38
NEG_MASK = -1.0e30
TILES = [(0, 128), (128, 128), (256, 128), (384, 128), (512, 16), (528, 32)]
PTILES = TILES[:5]
KW = [min(c + 128, RP) for c, _ in PTILES]

USES = (73, 72)
QH, GA, GATES, CONV, AO, WO, MLP = -1, 0, 1, 5, 6, 7, 8
ORDER = (4, 0, 1, 2, 3)


def phase_use(s, ph):
    return (9, 8)[s] + 4 * ph


def gate_use(k, c):
    return k % 2, c * 2 + (phase_use(k % 2, GATES) + k // 2)


def keys(r):
    return (KW[r] + P - 1) // P


def apart(eng, started):
    eng.sem_inc(started, 1)


class Chain:

    def __init__(self, eng, sem, started):
        self.eng, self.sem, self.started, self.base, self.k = eng, sem, started, 0, 0

    def link(self, ins, alone=False):
        ins.then_inc(self.sem, 1)
        self.k += 1
        self.eng.wait_ge(self.sem, self.base + self.k)
        if alone:
            apart(self.eng, self.started)

    def wait(self, behind=0):
        self.eng.wait_ge(self.sem, self.base + self.k - behind)
        apart(self.eng, self.started)

    def count(self, ins):
        ins.then_inc(self.sem, 1)
        self.k += 1

    @contextmanager
    def fori(self, n, per):
        apart(self.eng, self.started)
        with self.eng.Fori(0, n) as i:
            base, k = self.base, self.k
            self.base, self.k = base + k + i * per, 0
            yield i
            assert self.k == per, (self.k, per)
        self.base, self.k = base, k + n * per


def trunk_program(nc, a):
    with ExitStack() as ctx:
        def sb(name, shape, dt):
            return ctx.enter_context(nc.sbuf_tensor(name, shape, dt))

        def arena(name, nbytes):
            off = (nc.sbuf_base + 31) // 32 * 32
            sb(name, [P, nbytes // 4], F32)
            return off

        def at(name, shape, dt, off):
            return nc.alloc_sbuf_tensor_at(name, shape, dt, offset=off)

        BIG = KC * R * 4
        X = sb("X", [P, KC, R], F32)
        off_axh, off_axl, off_ahh, off_ahl = (arena(n, BIG) for n in ("r_axh", "r_axl", "r_ahh", "r_ahl"))
        AXh, AXl = at("AXh", [P, KC, R], F32R, off_axh), at("AXl", [P, KC, R], F32R, off_axl)
        AHh, AHl = at("AHh", [P, KC, R], F32R, off_ahh), at("AHl", [P, KC, R], F32R, off_ahl)
        KVB = [[at(f"KVB{h}{b4}", [P, TPP // 2, KV_W], F32, (off_axh, off_axl, off_ahh, off_ahl)[2 * h + b4 // 2]
                   + b4 % 2 * (TPP // 2 * KV_W * 4)) for b4 in range(4)] for h in range(2)]
        IKB = [at(f"IKB{g}", [P, 4, TPP, ID], F32, o) for g, o in enumerate((off_ahh, off_ahl))]
        RELU_S = [at(f"RELU_S{g}", [P, KEYS_S], F32, o) for g, o in enumerate((off_ahh, off_ahl))]
        off_q = arena("r_q", BIG)
        Q = at("Q", [P, KC, R], F32, off_q)
        SD = at("SD", [P, R], F32, off_q)
        RSTD = at("RSTD", [P, R], F32, off_q + 4 * R)
        XS, SS = at("XS", [P, R], F32, off_q + 8 * R), at("SS", [P, R], F32, off_q + 12 * R)
        off_sg = arena("r_sg", BIG)
        SG = at("SG", [P, KC, R], F32, off_sg)
        QI = at("QI", [P, 4, R], F32, off_sg)
        QIl = at("QIl", [P, 4, R], F32R, off_sg)
        KIT = [at(f"KIT{i}", [P, 512], F32, off_sg + 4 * 4 * R + i * 2048) for i in range(4)]
        SQ = at("SQ", [P, KC, R], F32, off_sg)
        off_bb = arena("r_bb", BIG)
        BB = at("BB", [P, KC, R], F32, off_bb)
        TK, o = [None], off_bb
        for r in range(1, 5):
            TK.append(at(f"TK{r}", [P, KW[r]], F32, o))
            o += 4 * KW[r]
        KNS = [at(f"KNS{i}", [P, KV_W], F32, o + 1024 * i) for i in range(2)]
        RELU_P = [at(f"RELU_P{i}", [P, RP], F32, o + 2048 + 2112 * i) for i in range(2)]
        ROPE = at("ROPE", [P, R], F32, o + 2048 + 4224)
        KDh = at("KDh", [P, RP], F32R, o + 2048 + 4224 + 4 * R)
        off_u = arena("r_u", 14528)
        UE = at("UE", [P, UE_W], F32, off_u)
        CY = at("CY", [P, R], F32, off_u + 2336)
        ICOS, ISIN = at("ICOS", [P, R], F32, off_u), at("ISIN", [P, R], F32, off_u + 2240)
        QCOS, QSIN = at("QCOS", [32, R], F32, off_u + 4480), at("QSIN", [32, R], F32, off_u + 6720)
        KI, KD = at("KI", [P, R], F32, off_u + 8960), at("KD", [P, R], F32, off_u + 11200)
        KDl = at("KDl", [P, R], F32R, off_u + 11200)
        QS = at("QS", [P, NB, IH, NS], F32, off_u + 13440)
        QST = at("QST", [P, RP], F32, off_u + 4576)
        PP = [at(f"PP{i}", [P, RP], F32, off_u + 6688 + 2112 * i) for i in range(2)]
        PPT = [at(f"PPT{i}", [P, w], F32, off_u + 10912 + 2048 * i) for i, w in enumerate((512, 384))]
        MS = at("MS", [RS, KEYS_S], BF16, off_u)
        QP = at("QP", [P, NB, KVH, HEADS, NS], F32, off_u + 4160)
        KTR = [at(f"KTR{i}", [P, 512], F32, off_u + 6208 + 2048 * i) for i in range(4)]
        MT = [at(f"MT{i}", [P, R], F32, off_u + 2240 * i) for i in range(4)]
        NAT = [at(f"NAT{i}", [P, DM], F32, off_u + 4096 * i) for i in range(2)]
        ST = [sb(f"ST{s}", [P, KC, P], F32) for s in range(2)]
        WH = [sb(f"WH{s}", [P, KC, P], F32R) for s in range(2)]
        WL = [sb(f"WL{s}", [P, KC, P], F32R) for s in range(2)]
        KT = sb("KT", [P, KVH, R], F32)
        VN = sb("VN", [P, 6, KV_W], F32)
        off_m = arena("r_m", 2 * sum(KW[1:]) + 4 * KEYS_S)
        MP, o = [None], off_m
        for r in range(1, 5):
            MP.append(at(f"MP{r}", [P, KW[r]], BF16, o))
            o += 2 * KW[r]
        TKS = at("TKS", [RS, KEYS_S], F32, o)
        PS_S = at("PS_S", [P, KEYS_S], F32, off_m)
        O_S = at("O_S", [P, KV_W], F32, off_m + 8320)
        VT = at("VT", [P, KVH, R], F32, off_m)
        PALL = at("PALL", [P, P], F32, off_m + 1024)
        SCN = at("SCN", [P, P], F32, off_m + 2 * 4 * R)
        QIh = [at(f"QIh{c}", [P, RP], F32R, off_m + (8 * R + 4 * P + 4 * RP * c if c < 3 else 0)) for c in range(4)]
        SELF = at("SELF", [RS, 2, P], F32, off_m)
        off_w = arena("r_w", 6 * (ID + IH) * 4)
        WKN = at("WKN", [P, 6, ID + IH], F32, off_w)
        CSN = at("CSN", [P, 2, P], F32, off_w)
        ident = sb("ident", [P, P], F32)
        identb = sb("identb", [P, P], BF16)
        caus = sb("caus", [P, P], F32)
        causb = sb("causb", [P, P], BF16)
        ones = sb("ones", [P, P], F32)
        selb = sb("selb", [RS, 2, P], BF16)
        expand = sb("expand", [P, P], F32)
        pick = sb("pick", [P, 2, RS], F32)
        newok = sb("newok", [RS, RS], F32)
        PTT = sb("PTT", [P, 112], F32)
        PL = sb("PL", [P, 56], F32)
        SCT = sb("SCT", [P, P], F32)
        CSO = sb("CSO", [P, 18, KC], F32)
        WIB = sb("WIB", [P, 2, RS], F32)
        PTB = sb("PTB", [P, NB], I32)
        SEG = sb("SEG", [P, 1], F32)
        IDX = sb("IDX", [P, NB], U32)
        IDXH = sb("IDXH", [P, 2, NB], U32)
        top = sb("top", [P, 4, 8], F32)
        st = sb("st", [P, 16], F32)
        stp = sb("stp", [P, 2, 4], F32)
        eps, one = sb("eps", [P, 1], F32), sb("one", [P, 1], F32)
        PS = [ctx.enter_context(nc.psum_tensor(f"PS{s}", [P, 2, 512], F32)) for s in range(2)]
        PB = ctx.enter_context(nc.psum_tensor("PB", [P, 4, 512], F32))

        def sem(name):
            return ctx.enter_context(nc.semaphore(name))

        loaded = [sem(f"loaded{s}") for s in range(2)]
        hi_done = [sem(f"hi_done{s}") for s in range(2)]
        lo_done = [sem(f"lo_done{s}") for s in range(2)]
        mm_done = [sem(f"mm_done{s}") for s in range(2)]
        evac_done = [sem(f"evac_done{s}") for s in range(2)]
        started = sem("started")
        a_ready = sem("a_ready")
        dve_own = sem("dve_own")
        const_in, x_in = sem("const_in"), [sem(f"x_in{i}") for i in range(2)]
        setup_t, setup_e = sem("setup_t"), sem("setup_e")
        params_t = sem("params_t")
        idx_ready, tables_in, state_in, ik_in = sem("idx_ready"), sem("tables_in"), sem("state_in"), sem("ik_in")
        ki_ready, kv_ready, q_ready = sem("ki_ready"), sem("kv_ready"), sem("q_ready")
        qi_split = sem("qi_split")
        ki_t, ki_e, wi_mm, wib_ready = sem("ki_t"), sem("ki_e"), sem("wi_mm"), sem("wib_ready")
        kv_t, kv_e = sem("kv_t"), sem("kv_e")
        out_small = sem("out_small")
        out_k, out_v = [sem(f"out_k{i}") for i in range(2)], sem("out_v")
        sc_mm, sc_relu, sc_acc = sem("sc_mm"), sem("sc_relu"), sem("sc_acc")
        kit_t, kit_e, ss_step, ss_mm, ss_relu = (sem("kit_t"), sem("kit_e"), sem("ss_step"), sem("ss_mm"),
                                                 sem("ss_relu"))
        w_mm, tks_past, tks_ready, ue_init = sem("w_mm"), sem("tks_past"), sem("tks_ready"), sem("ue_init")
        cso_ready, cso_t, cso_e, out_c = sem("cso_ready"), sem("cso_t"), sem("cso_e"), sem("out_c")
        mp_ready = sem("mp_ready")
        inv_done = sem("inv_done")
        masks_ready, qp_ready = sem("masks_ready"), sem("qp_ready")
        kv_in = [[sem(f"kv_in{h}{b4}") for b4 in range(4)] for h in range(2)]
        kt_t, kt_ea, kt_ed, kt_mm = sem("kt_t"), sem("kt_ea"), sem("kt_ed"), sem("kt_mm")
        ls_mm, ls_max, ls_exp = sem("ls_mm"), sem("ls_max"), sem("ls_exp")
        pt_t, pt_e, pv_mm, os_e, ot_t, ot_e = (sem("pt_t"), sem("pt_e"), sem("pv_mm"), sem("os_e"),
                                               sem("ot_t"), sem("ot_e"))
        qst_done, lp_mm, lp_max = sem("qst_done"), sem("lp_mm"), sem("lp_max")
        lp_exp, lp_inv, pp_norm = sem("lp_exp"), sem("lp_inv"), sem("pp_norm")
        pp_t, pp_e, op_mm, op_e = sem("pp_t"), sem("pp_e"), sem("op_mm"), sem("op_e")
        relu_h = sem("relu_h")
        xs_ready, ln_red, ln_hi = sem("xs_ready"), sem("ln_red"), sem("ln_hi")
        ln_sum, ln_dev, ln_sq, ln_var, ln_sd, ln_norm, ln_aff = (sem("ln_sum"), sem("ln_dev"), sem("ln_sq"),
                                                                sem("ln_var"), sem("ln_sd"), sem("ln_norm"), sem("ln_aff"))
        y_t, y_e, out_y = sem("y_t"), sem("y_e"), [sem(f"out_y{i}") for i in range(2)]

        block = ctx.enter_context(nc.Block())

        w_in_v = a["w_in"].rearrange("l (c p) n -> l p c n", p=P)
        w_views = {n: a[n].rearrange("l (c p) n -> l p c n", p=P) for n in ("w_attn_out", "w_conv_out", "w_o", "w_up")}
        w_down_v = a["w_down"].rearrange("l (g c p) n -> (l g) p c n", g=NG, p=P)
        rows_k = a["cache_k"].rearrange("l n (s t) h d -> (l n s) (t h d)", t=TPP // 2)
        rows_v = a["cache_v"].rearrange("l n (s t) h d -> (l n s) (t h d)", t=TPP // 2)
        rows_ik = a["cache_idx_k"].rearrange("l n (s t) d -> (l n s) (t d)", t=TPP)
        n_rows = a["cache_k"].shape[1] * (PAGE // TPP)

        def rope_swap(half):
            return [(j + half) % (2 * half) if j < 2 * half else j for j in range(32)]

        @block.sync
        def _(sp):
            def load(s, n, src):
                sp.wait_ge(lo_done[s], n + 1)
                sp.dma_start(ST[s][:, :, :], src).then_inc(loaded[s], 16)

            def wcol(v, l, col):
                return v[bass.ds(l, 1), :, :, bass.ds(col, P)].rearrange("o p c n -> (o p) c n")

            with nc.allow_non_contiguous_dma(reason="page ids, one word each"):
                for j in range(NPG):
                    sp.dma_start(PTB[8 * j:8 * j + 8, :],
                                 a["page_table"][:, j:j + 1].rearrange("b j -> j b").to_broadcast([8, NB])
                                 ).then_inc(const_in, 16)
            for t, n in ((ident, "c_ident"), (caus, "c_caus"), (expand, "c_expand"), (pick, "c_pick"),
                         (newok, "c_newok"), (SEG, "c_seg"), (SELF, "c_sel")):
                sp.dma_start(t[:], a[n]).then_inc(const_in, 16)
            for l in range(DEPTH):
                for j, n in enumerate(("ln1_g", "ln1_b", "ln2_g", "ln2_b")):
                    sp.dma_start(PALL[56 * l + 8 * j:56 * l + 8 * j + 8, :],
                                 a[n][l].rearrange("(c d) -> c d", d=P)).then_inc(const_in, 16)
                sp.dma_start(PALL[56 * l + 32:56 * l + 56, :],
                             a["conv_w"][l].rearrange("j (c d) -> (j c) d", d=P)).then_inc(const_in, 16)
            for s in range(2):
                load(s, 0, w_in_v[0, :, :, COL_QI + P * s:COL_QI + P * s + P])
            srcs = [(a["meta_tokens"], 16)] + [(a["x_prompt"][0, P * t:P * t + P, :], P) for t in range(4)]
            srcs += [(a["x_sample"].rearrange("b s d -> (b s) d"), RS)]
            for t, (src, n) in enumerate(srcs):
                if t >= 2:
                    sp.wait_ge(setup_t, t - 1)
                sp.dma_start(NAT[t % 2][0:n, :], src).then_inc(x_in[t % 2], 16)

            with sp.Fori(0, DEPTH) as l:
                def use(s, n):
                    return l * USES[s] + n

                load(0, use(0, 1), wcol(w_in_v, l, COL_QI + 2 * P))
                load(1, use(1, 1), wcol(w_in_v, l, COL_QI + 3 * P))
                load(0, use(0, 2), wcol(w_in_v, l, COL_KI))
                load(1, use(1, 2), wcol(w_in_v, l, COL_K + P))
                load(0, use(0, 3), wcol(w_in_v, l, COL_K))
                load(0, use(0, 4), wcol(w_in_v, l, COL_V))
                load(1, use(1, 3), wcol(w_in_v, l, COL_V + P))
                with sp.Fori(0, 4) as i:
                    for s in range(2):
                        load(s, l * USES[s] + (phase_use(s, QH) + i), wcol(w_in_v, l, COL_Q + s * P + i * (2 * P)))
                with sp.Fori(0, 4) as i:
                    for s in range(2):
                        load(s, l * USES[s] + (phase_use(s, GA) + i), wcol(w_in_v, l, COL_GA + s * P + i * (2 * P)))
                with sp.Fori(0, KC) as c:
                    for k, col in enumerate((COL_H, COL_CG, COL_BG, COL_GB)):
                        s, n = gate_use(k, c)
                        load(s, l * USES[s] + n, wcol(w_in_v, l, c * P + col))
                for name, ph in (("w_conv_out", CONV), ("w_attn_out", AO), ("w_o", WO)):
                    with sp.Fori(0, 4) as i:
                        for s in range(2):
                            load(s, l * USES[s] + (phase_use(s, ph) + i), wcol(w_views[name], l, s * P + i * (2 * P)))
                with sp.Fori(0, NG) as g:
                    with sp.Fori(0, 4) as i:
                        for s in range(2):
                            load(s, l * USES[s] + g * 8 + i + phase_use(s, MLP),
                                 wcol(w_views["w_up"], l, g * DM + i * (2 * P) + s * P))
                    with sp.Fori(0, 4) as i:
                        for s in range(2):
                            load(s, l * USES[s] + g * 8 + i + phase_use(s, MLP + 1),
                                 wcol(w_down_v, l * NG + g, i * (2 * P) + s * P))
                for s in range(2):
                    load(s, use(s, USES[s]), wcol(w_in_v, (l + 1) % DEPTH, COL_QI + P * s))
            for s in range(2):
                sp.wait_ge(loaded[s], 16 * (DEPTH * USES[s] + 1))

        @block.gpsimd
        def _(pool):
            def rest(s, n):
                pool.wait_ge(hi_done[s], n + 1)
                pool.tensor_tensor(WL[s][:, :, :], ST[s][:, :, :], WH[s][:, :, :].bitcast(F32),
                                   ALU.subtract).then_inc(lo_done[s], 1)

            for s in range(2):
                pool.sem_inc(lo_done[s], 1)
            for s in range(2):
                rest(s, 0)
            with pool.Fori(0, DEPTH) as l:
                pool.wait_ge(a_ready, l * 72 + 8)
                apart(pool, started)
                for n, t in (("c_icos", ICOS), ("c_isin", ISIN), ("c_qcos", QCOS), ("c_qsin", QSIN)):
                    pool.dma_start(t[:, :], a[n]).then_inc(tables_in, 16)
                pool.dma_start(SCN[:, :], a["state_conv"][bass.ds(l, 1)].rearrange("o b t (c d) -> (o b t c) d", d=P)
                               ).then_inc(state_in, 16)
                pool.wait_ge(idx_ready, l + 1)
                apart(pool, started)
                for b in range(NB):
                    pool.indirect_dma_start(IKB[b // 4][:, b % 4].rearrange("p t d -> p (t d)"), None, rows_ik,
                                            bass.IndirectOffsetOnAxis(ap=IDX[:, b:b + 1], axis=0)
                                            ).then_inc(ik_in, 16)
                for s, n in ((0, 1), (1, 1), (0, 2), (1, 2), (0, 3), (0, 4), (1, 3)):
                    rest(s, l * USES[s] + n)
                with pool.Fori(0, 4 * (CONV + 1)) as i:
                    for s in range(2):
                        rest(s, l * USES[s] + i + phase_use(s, QH))
                for s in range(2):
                    rest(s, l * USES[s] + phase_use(s, CONV))

                def gather(g, h, rows):
                    for b4 in range(4):
                        b = 4 * g + b4
                        pool.indirect_dma_start(KVB[h][b4][:].rearrange("p t d -> p (t d)"), None, rows,
                                                bass.IndirectOffsetOnAxis(ap=IDXH[:, h, b:b + 1], axis=0)
                                                ).then_inc(kv_in[h][b4], 16)

                def products_done(ph):
                    for s in range(2):
                        pool.wait_ge(mm_done[s], l * USES[s] + phase_use(s, ph) + 1)
                        apart(pool, started)

                products_done(CONV)
                gather(0, 0, rows_k)
                with pool.Fori(0, 3) as i:
                    for s in range(2):
                        rest(s, l * USES[s] + i + (phase_use(s, CONV) + 1))
                for s in range(2):
                    rest(s, l * USES[s] + phase_use(s, AO))
                products_done(AO)
                gather(0, 1, rows_k)
                for g in range(2):
                    if g == 1:
                        for h in range(2):
                            pool.wait_ge(pv_mm, l * 10 + 2 * h + 2)
                            apart(pool, started)
                            gather(1, h, rows_k)
                    for h in range(2):
                        pool.wait_ge(kt_t, l * 64 + 32 * g + 16 * h + 16)
                        apart(pool, started)
                        gather(g, h, rows_v)
                with pool.Fori(0, 3) as i:
                    for s in range(2):
                        rest(s, l * USES[s] + i + (phase_use(s, AO) + 1))
                with pool.Fori(0, 4 + 4 * 2 * NG) as i:
                    for s in range(2):
                        rest(s, l * USES[s] + i + phase_use(s, WO))
                for s in range(2):
                    rest(s, l * USES[s] + USES[s])

        @block.tensor
        def _(pe):
            for s in range(2):
                pe.sem_inc(mm_done[s], 1)

            def unit(s, n, hi, lo, ready=None, first=True, last=True):
                pe.wait_ge(lo_done[s], n + 2)
                pe.wait_ge(evac_done[s], n + 1)
                for k in range(KC):
                    if ready is not None:
                        pe.wait_ge(a_ready, ready + k)
                    for x, y in ((WH[s], hi), (WL[s], hi), (WH[s], lo)):
                        for h in range(2):
                            mm = pe.matmul(PS[s][:, h, 0:RH], x[:, k, :], y[:, k, RH * h:RH * h + RH],
                                           start=(k == 0 and y is hi and x is WH[s]),
                                           stop=(k == KC - 1 and y is lo))
                mm.then_inc(mm_done[s], 1)

            pe.wait_ge(const_in, 16 * (NPG + 7 + 10))
            for t, (c0, n) in enumerate([(0, 16)] + [(16 + P * j, P) for j in range(4)] + [(RP, RS)]):
                pe.wait_ge(x_in[t % 2], 16 * (t // 2 + 1))
                if t >= 2:
                    pe.wait_ge(setup_e, t - 1)
                for c in range(KC):
                    tr = pe.transpose(PS[t % 2][:, c // 4, P * (c % 4):P * (c % 4) + n],
                                      NAT[t % 2][0:n, P * c:P * c + P], ident[0:n, 0:n])
                tr.then_inc(setup_t, 1)
            pe.transpose(PB[:, 0, 0:112], PALL[0:112, :], ident[0:112, 0:112]).then_inc(params_t, 1)
            pe.wait_ge(setup_e, 6)

            apart(pe, started)
            with pe.Fori(0, DEPTH) as l:
                def use(s, n):
                    return l * USES[s] + n

                x0 = l * 72 + 1
                for s, n in ((0, 0), (1, 0), (0, 1), (1, 1), (0, 2), (0, 3), (1, 2), (0, 4), (1, 3)):
                    unit(s, use(s, n), AXh, AXl, ready=x0 if n == 0 else None)
                apart(pe, started)
                with pe.Fori(0, 4) as i:
                    for s in range(2):
                        unit(s, l * USES[s] + i + phase_use(s, QH), AXh, AXl)

                pe.wait_ge(ki_ready, l + 1)
                apart(pe, started)
                for t, (c0, n) in enumerate(TILES):
                    tr = pe.transpose(PB[0:n, 0, 80 * t:80 * t + 72], KI[0:72, c0:c0 + n], ident[0:72, 0:72])
                tr.then_inc(ki_t, 1)
                pe.matmul(PB[:, 1, 0:RS], expand[ID:ID + IH, :], KI[ID:ID + IH, RP:R], start=True, stop=True)
                pe.wait_ge(state_in, l * 16 + 16)
                pe.transpose(PB[:, 1, P:2 * P], SCN[:, :], ident[:, :]).then_inc(wi_mm, 1)
                pe.wait_ge(kv_ready, l + 1)
                pe.wait_ge(evac_done[1], use(1, 4) + 1)
                pe.wait_ge(evac_done[0], use(0, 5) + 1)
                for t, (c0, n) in enumerate(TILES):
                    if t >= 2:
                        pe.wait_ge(kv_e, l * 6 + t - 1)
                    for h in range(KVH):
                        pe.transpose(PB[0:n, 2 + t % 2, P * h:P * h + P], KT[:, h, c0:c0 + n], ident[:, :])
                        tr = pe.transpose(PB[0:n, 2 + t % 2, 256 + P * h:256 + P * h + P], VT[:, h, c0:c0 + n],
                                          ident[:, :])
                    tr.then_inc(kv_t, 1)

                pe.wait_ge(qi_split, l * 2 + 1)
                for s in range(2):
                    pe.wait_ge(evac_done[s], use(s, (9, 8)[s]) + 1)
                j = 0
                for r in range(1, 5):
                    c0, n = PTILES[r]
                    for h in range(IH):
                        if j >= 2:
                            pe.wait_ge(sc_relu, l * 32 + j - 1)
                            apart(pe, started)
                        if j == 6:
                            pe.wait_ge(qi_split, l * 2 + 2)
                            apart(pe, started)
                        hp = slice(ID * (h % 2), ID * (h % 2) + ID)
                        for k0 in range(0, KW[r], 512):
                            k1 = min(k0 + 512, KW[r])
                            for i, (x, y) in enumerate(((QIh[h // 2], KDh), (QIl[:, h // 2], KDh), (QIh[h // 2], KDl))):
                                mm = pe.matmul(PS[j % 2][0:n, k0 // 512, 0:k1 - k0], x[hp, c0:c0 + n], y[hp, k0:k1],
                                               start=(i == 0), stop=(i == 2))
                        mm.then_inc(sc_mm, 1)
                        j += 1

                pe.wait_ge(ik_in, (l + 1) * (16 * NB))
                pe.wait_ge(ki_e, l + 1)
                pe.wait_ge(wib_ready, l + 1)
                pe.wait_ge(kv_e, l * 6 + 6)
                pe.wait_ge(sc_relu, l * 32 + 32)

                def ik_transposes(t):
                    g, jh, j = t // 8, t // 4 % 2, t % 4
                    if t >= 4:
                        pe.wait_ge(kit_e, l * 16 + t - 3)
                    for i in range(4):
                        tok = 8 * jh + 2 * i
                        tr = pe.transpose(PB[:, j, P * i:P * i + P],
                                          IKB[g][:, j, tok:tok + 2, :].rearrange("p t d -> p (t d)"), ident[:, :])
                    tr.then_inc(kit_t, 1)

                for t in range(4):
                    ik_transposes(t)
                for q in range(4):
                    g, jh = q // 2, q % 2
                    pe.wait_ge(kit_e, l * 16 + 4 * q + 4)
                    apart(pe, started)
                    if q == 2:
                        pe.wait_ge(ss_relu, l * 3 + 1)
                        apart(pe, started)
                    for par in range(2):
                        for j in range(4):
                            mm = pe.matmul(PS[par][32 * j:32 * j + 32, jh, :],
                                           QS[ID * par:ID * par + ID, 4 * g + j].rearrange("p h s -> p (h s)"),
                                           KIT[j][ID * par:ID * par + ID, :], start=True, stop=True)
                    mm.then_inc(ss_step, 1)
                    if q < 3:
                        for t in range(4 * q + 4, 4 * q + 8):
                            ik_transposes(t)
                for b in range(NB):
                    b4 = 32 * (b % 4)
                    mm = pe.matmul(PB[b4:b4 + 32, 0, 32 * (b // 4):32 * (b // 4) + 32],
                                   QS[0:ID, b].rearrange("p h s -> p (h s)"), KD[0:ID, RP:R], start=True, stop=True)
                mm.then_inc(ss_mm, 1)
                pe.wait_ge(ss_relu, l * 3 + 3)
                apart(pe, started)
                for par in range(2):
                    for jh in range(2):
                        col = 512 * (2 * par + jh)
                        for g in range(2):
                            pe.matmul(PS[par][0:RS, jh, :], WIB[:, g, :], RELU_S[g][:, col:col + 512],
                                      start=(g == 0), stop=(g == 1))
                for g in range(2):
                    mm = pe.matmul(PB[0:RS, 1, 0:RS], WIB[:, g, :], RELU_S[g][:, PAST:KEYS_S],
                                   start=(g == 0), stop=(g == 1))
                mm.then_inc(w_mm, 1)

                pe.wait_ge(tks_past, l + 1)
                apart(pe, started)
                with pe.Fori(0, 4) as i:
                    for s in range(2):
                        unit(s, l * USES[s] + i + phase_use(s, GA), AXh, AXl)

                pe.wait_ge(tks_ready, l + 1)
                pe.wait_ge(mp_ready, l + 1)
                for n in range(KVH):
                    apart(pe, started)
                    with pe.Fori(0, GRP) as i:
                        c = i + GRP * n
                        H = l * HEADS + c

                        def gate(k):
                            s, u = gate_use(k, c)
                            unit(s, l * USES[s] + u, AXh, AXl)

                        def p_logits(i):
                            r = ORDER[i]
                            c0, m = PTILES[r]
                            pe.wait_ge(lp_exp, H * 5 + 2 + (0, 1, 1, 2, 3)[i])
                            apart(pe, started)
                            msk = causb if r == 0 else MP[r]
                            for k0 in range(0, KW[r], 512):
                                k1 = min(k0 + 512, KW[r])
                                bank = PB[0:m, (0, 0, 1, 0, 1)[i] + k0 // 512, 0:k1 - k0]
                                pe.matmul(bank, identb[0:m, 0:m], msk[0:m, k0:k1], start=True, stop=False)
                                mm = pe.matmul(bank, QST[:, c0:c0 + m], KT[:, n, k0:k1], start=False, stop=True)
                            mm.then_inc(lp_mm, 1)

                        def p_transposes(i):
                            r = ORDER[i]
                            m = PTILES[r][1]
                            pe.wait_ge(pp_norm, H * 5 + i + 1)
                            if i > 0:
                                pe.wait_ge(pp_e, H * 5 + i)
                            apart(pe, started)
                            for kt in range(keys(r)):
                                k1 = min(P, KW[r] - P * kt)
                                tr = pe.transpose(PB[0:k1, 2, m * kt:m * kt + m], PP[i % 2][0:m, P * kt:P * kt + k1],
                                                  ident[0:m, 0:m])
                            tr.then_inc(pp_t, 1)

                        def p_values(i):
                            r = ORDER[i]
                            m = PTILES[r][1]
                            pe.wait_ge(pp_e, H * 5 + i + 1)
                            pe.wait_ge(op_e, H * 5 + i + 2)
                            apart(pe, started)
                            for kt in range(keys(r)):
                                k1 = min(P, KW[r] - P * kt)
                                mm = pe.matmul(PB[:, 3, 0:m], VN[0:k1, kt, HD * n:HD * n + HD],
                                               PPT[i % 2][0:k1, m * kt:m * kt + m], start=(kt == 0),
                                               stop=(kt == keys(r) - 1))
                            mm.then_inc(op_mm, 1)

                        pe.wait_ge(qst_done, l * (HEADS + 1) + c + 1)
                        p_logits(0)
                        gate(0)
                        p_transposes(0)
                        p_logits(1)
                        p_logits(2)
                        gate(1)
                        p_transposes(1)
                        p_logits(3)
                        p_values(0)
                        p_transposes(2)
                        p_values(1)
                        gate(2)
                        p_logits(4)
                        p_transposes(3)
                        p_values(2)
                        gate(3)
                        p_transposes(4)
                        p_values(3)
                        p_values(4)
                pe.wait_ge(op_e, l * 40 + 42)
                pe.wait_ge(cso_ready, l + 1)
                pe.transpose(PB[:, 0, 0:P], CSO[:, 0:16, :].rearrange("p r c -> p (r c)"), ident[:, :])
                pe.transpose(PB[0:16, 0, P:2 * P], CSO[:, 16:18, :].rearrange("p r c -> p (r c)"),
                             ident[:, :]).then_inc(cso_t, 1)
                apart(pe, started)
                with pe.Fori(0, 4) as i:
                    for s in range(2):
                        unit(s, l * USES[s] + i + phase_use(s, CONV), AHh, AHl, ready=l * 72 + 9 if s == 0 else None)

                pe.wait_ge(qp_ready, l + 1)
                pe.wait_ge(cso_e, l + 1)
                for s in range(2):
                    pe.wait_ge(evac_done[s], use(s, phase_use(s, AO)) + 1)
                banks = [PS[0][:, 0, :], PS[0][:, 1, :], PS[1][:, 0, :]]
                new_l = PS[1][:, 1, 0:RS]
                out_s = PS[1][:, 1, KV_W:2 * KV_W]
                for g in range(2):
                    def evacuated(t):
                        pe.wait_ge((kt_ea, kt_ed)[t % 2], l * 32 + 16 * g + t // 2 + 1)

                    def k_transposes(t):
                        q, b4 = t // 4, t % 4
                        c, n = q // KVH, q % KVH
                        if q in (0, 4):
                            pe.wait_ge(kv_in[q // 4][b4], l * 64 + 32 * g + 16)
                        if t >= 3:
                            evacuated(t - 3)
                        for j in range(4):
                            tr = pe.transpose(banks[t % 3][:, P * j:P * j + P],
                                              KVB[c // 2][b4][:, 4 * (c % 2) + j, HD * n:HD * n + HD], ident[:, :])
                        tr.then_inc(kt_t, 1)

                    for t in range(3):
                        k_transposes(t)
                    for q in range(8):
                        c, n = q // KVH, q % KVH
                        for t in range(4 * q + 3, min(4 * q + 7, 32)):
                            k_transposes(t)
                        evacuated(4 * q + 2)
                        evacuated(4 * q + 3)
                        for b4 in range(4):
                            mm = pe.matmul(PB[32 * b4:32 * b4 + 32, c, :],
                                           QP[:, 4 * g + b4, n].rearrange("p h s -> p (h s)"), KTR[b4][:, :],
                                           start=(n == 0), stop=False)
                        mm.then_inc(kt_mm, 1)
                        if n == KVH - 1:
                            if g == 0 and c == 0:
                                pe.wait_ge(masks_ready, l + 1)
                                apart(pe, started)
                            pe.matmul(PB[:, c, :], selb[:, g, :], MS[:, 512 * c:512 * c + 512], start=False,
                                      stop=True).then_inc(ls_mm, 1)
                        if q == 3:
                            if g == 1:
                                pe.wait_ge(ot_e, l * 2 + 1)
                                apart(pe, started)
                            for b4 in range(4):
                                for m in range(KVH):
                                    pe.matmul(new_l[32 * b4:32 * b4 + 32, :],
                                              QP[:, 4 * g + b4, m].rearrange("p h s -> p (h s)"),
                                              KT[:, m, RP:R], start=(m == 0), stop=False)
                            pe.matmul(new_l, selb[:, g, :], MS[:, PAST:KEYS_S], start=False, stop=True).then_inc(ls_mm, 1)

                    def pt_transposes(c):
                        w, kn = (4, P) if c < 4 else (1, RS)
                        pe.wait_ge(ls_exp, l * 10 + 5 * g + (c + 2 if c < 4 else 1))
                        if c >= 3:
                            pe.wait_ge(pt_e, l * 10 + 5 * g + c - 2)
                        for j in range(w):
                            tr = pe.transpose(banks[c % 3][0:kn, P * j:P * j + P],
                                              PS_S[:, 512 * c + P * j:512 * c + P * j + kn], ident[:, :])
                        tr.then_inc(pt_t, 1)

                    for c in range(3):
                        pt_transposes(c)
                    for c in range(5):
                        w, kn = (4, P) if c < 4 else (1, RS)
                        pe.wait_ge(pt_e, l * 10 + 5 * g + c + 1)
                        apart(pe, started)
                        for j in range(w):
                            for b4 in range(4):
                                if c in (0, 2) and j == 0:
                                    pe.wait_ge(kv_in[c // 2][b4], l * 64 + 32 * g + 32)
                                pt = KTR[c % 4][0:kn, P * j + 32 * b4:P * j + 32 * b4 + 32]
                                vv = KVB[c // 2][b4][:, 4 * (c % 2) + j, :] if c < 4 else VN[0:RS, 5, :]
                                mm = pe.matmul(out_s[32 * b4:32 * b4 + 32, :], pt, vv,
                                               start=(c == 0 and j == 0), stop=(c == 4))
                        mm.then_inc(pv_mm, 1)
                        if c + 3 < 5:
                            pt_transposes(c + 3)
                    pe.wait_ge(os_e, l * 2 + g + 1)
                    for n in range(KVH):
                        tr = pe.transpose(PS[1][:, 1, P * n:P * n + P], O_S[:, HD * n:HD * n + HD], ident[:, :])
                    tr.then_inc(ot_t, 1)

                apart(pe, started)
                with pe.Fori(0, 4) as i:
                    for s in range(2):
                        unit(s, l * USES[s] + i + phase_use(s, AO), AXh, AXl, ready=l * 72 + 17 if s == 0 else None)
                apart(pe, started)
                with pe.Fori(0, 4) as i:
                    for s in range(2):
                        unit(s, l * USES[s] + i + phase_use(s, WO), AHh, AHl, ready=l * 72 + 25 if s == 0 else None)

                def layer_norm(j):
                    for s in range(2):
                        pe.wait_ge(evac_done[s], use(s, phase_use(s, MLP + 8 * j)) + 1)
                    pe.wait_ge(xs_ready, l * 2 + j + 1)
                    for h in range(2):
                        pe.matmul(PS[0][:, h, 0:RH], ones[:, :], XS[:, RH * h:RH * h + RH],
                                  start=True, stop=True).then_inc(ln_sum, 1)
                    for h in range(2):
                        pe.wait_ge(ln_red, l * 4 + 2 * j + h + 1)
                        pe.matmul(PS[1][:, h, 0:RH], ones[:, :], SS[:, RH * h:RH * h + RH],
                                  start=True, stop=True).then_inc(ln_var, 1)

                layer_norm(0)
                pe.wait_ge(ln_sd, l * 4 + 2)
                apart(pe, started)
                with pe.Fori(0, NG) as g:
                    apart(pe, started)
                    with pe.Fori(0, 4) as i:
                        for s in range(2):
                            unit(s, l * USES[s] + g * 8 + i + phase_use(s, MLP), AXh, AXl,
                                 ready=l * 72 + 33 if s == 0 else None)
                    apart(pe, started)
                    with pe.Fori(0, 4) as i:
                        for s in range(2):
                            unit(s, l * USES[s] + g * 8 + i + phase_use(s, MLP + 1), AHh, AHl,
                                 ready=l * 72 + g * 8 + 41 if s == 0 else None)
                layer_norm(1)
                pe.wait_ge(ln_sd, l * 4 + 4)

            pe.wait_ge(ln_aff, DEPTH * 2 * KC)
            for t, (c0, n) in enumerate([(16 + P * j, P) for j in range(4)] + [(RP, RS)]):
                if t >= 2:
                    pe.wait_ge(y_e, t - 1)
                for c in range(KC):
                    tr = pe.transpose(PS[t % 2][0:n, c // 4, P * (c % 4):P * (c % 4) + P], X[:, c, c0:c0 + n], ident[:, :])
                tr.then_inc(y_t, 1)

        @block.scalar
        def _(act):
            def high(s, n):
                act.wait_ge(loaded[s], n * 16 + 16)
                act.wait_ge(mm_done[s], n + 1)
                act.copy(WH[s][:, :, :], ST[s][:, :, :]).then_inc(hi_done[s], 1)

            def halves(dst):
                return dst.rearrange("p (h r) -> p h r", h=2)

            def evac(s, n, fn):
                high(s, n + 1)
                act.wait_ge(mm_done[s], n + 2)
                apart(act, started)
                fn().then_inc(evac_done[s], 1)

            for s in range(2):
                high(s, 0)
            act.wait_ge(const_in, 16 * (NPG + 7 + 10))
            act.copy(identb[:, :], ident[:, :])
            act.mul(causb[:, :], caus[:, :], NEG_MASK)
            act.copy(selb[:, :, :], SELF[:, :, :])
            for t, (c0, n) in enumerate([(0, 16)] + [(16 + P * j, P) for j in range(4)] + [(RP, RS)]):
                act.wait_ge(setup_t, t + 1)
                for hb in range(2):
                    e = act.copy(X[:, 4 * hb:4 * hb + 4, c0:c0 + n],
                                 PS[t % 2][:, hb, :].rearrange("p (c r) -> p c r", r=P)[:, :, 0:n])
                e.then_inc(setup_e, 1)

            apart(act, started)
            with act.Fori(0, DEPTH) as l:
                def use(s, n):
                    return l * USES[s] + n

                act.wait_ge(a_ready, l * 72 + 8)
                for s, n, dst in ((0, 0, QI[:, 0, :]), (1, 0, QI[:, 1, :]), (0, 1, QI[:, 2, :]), (1, 1, QI[:, 3, :]),
                                  (0, 2, KI[:, :]), (0, 3, KT[:, 0, :]), (1, 2, KT[:, 1, :]),
                                  (0, 4, VT[:, 0, :]), (1, 3, VT[:, 1, :])):
                    evac(s, use(s, n), lambda: act.copy(halves(dst), PS[s][:, :, 0:RH]))
                apart(act, started)
                with act.Fori(0, 4) as i:
                    for s in range(2):
                        evac(s, l * USES[s] + i + phase_use(s, QH),
                             lambda: act.copy(halves(Q[:, bass.ds(i * 2 + s, 1), :].rearrange("p o r -> p (o r)")),
                                              PS[s][:, :, 0:RH]))
                act.wait_ge(ki_t, l + 1)
                act.copy(WKN[:, 0:4, :], PB[:, 0, 0:320].rearrange("p (t d) -> p t d", t=4)[:, :, 0:72])
                act.copy(WKN[0:16, 4, :], PB[0:16, 0, 320:392])
                act.copy(WKN[0:RS, 5, :], PB[0:RS, 0, 400:472]).then_inc(ki_e, 1)
                act.wait_ge(ki_e, l + 1)
                act.dma_start(a["o_ik"][bass.ds(l, 1), 0, 0:512, :].rearrange("o (t p) d -> (o p) t d", p=P),
                              WKN[:, 0:4, 0:ID]).then_inc(out_small, 16)
                act.dma_start(a["o_ik"][bass.ds(l, 1), 0, 512:RP, :].rearrange("o p d -> (o p) d"),
                              WKN[0:16, 4, 0:ID]).then_inc(out_small, 16)
                act.dma_start(a["o_iks"][bass.ds(l, 1)].rearrange("o b s d -> (o b s) d"),
                              WKN[0:RS, 5, 0:ID]).then_inc(out_small, 16)
                for t, (c0, n) in enumerate(TILES):
                    act.wait_ge(kv_t, l * 6 + t + 1)
                    if t >= 2:
                        act.wait_ge(out_k[t % 2], l * 48 + 16 * (t // 2))
                    act.copy(KNS[t % 2][0:n, :], PB[0:n, 2 + t % 2, 0:256])
                    act.copy(VN[0:n, t, :], PB[0:n, 2 + t % 2, 256:512]).then_inc(kv_e, 1)
                    act.wait_ge(kv_e, l * 6 + t + 1)
                    apart(act, started)
                    if t < 5:
                        kd = a["o_k"][bass.ds(l, 1), 0, c0:c0 + n].rearrange("o r h d -> (o r) (h d)")
                        vd = a["o_v"][bass.ds(l, 1), 0, c0:c0 + n].rearrange("o r h d -> (o r) (h d)")
                    else:
                        kd = a["o_ks"][bass.ds(l, 1)].rearrange("o b s h d -> (o b s) (h d)")
                        vd = a["o_vs"][bass.ds(l, 1)].rearrange("o b s h d -> (o b s) (h d)")
                    act.dma_start(kd, KNS[t % 2][0:n, :]).then_inc(out_k[t % 2], 16)
                    act.dma_start(vd, VN[0:n, t, :]).then_inc(out_v, 16)
                act.wait_ge(q_ready, l + 1)
                j = 0
                for r in range(1, 5):
                    n = PTILES[r][1]
                    for h in range(IH):
                        act.wait_ge(sc_mm, l * 32 + j + 1)
                        if j >= 2:
                            act.wait_ge(sc_acc, l * 32 + j - 1)
                        act.activation(RELU_P[j % 2][0:n, 0:KW[r]],
                                       PS[j % 2][0:n].rearrange("p b k -> p (b k)")[:, 0:KW[r]],
                                       ACT.Relu).then_inc(sc_relu, 1)
                        j += 1
                def relu_group(g):
                    act.wait_ge(ss_step, l * 4 + 2 * g + 2)
                    for par in range(2):
                        e = act.activation(RELU_S[g][:, 1024 * par:1024 * par + 1024],
                                           PS[par][:, :, :].rearrange("p j t -> p (j t)"), ACT.Relu)
                    e.then_inc(ss_relu, 1)

                for t in range(16):
                    act.wait_ge(kit_t, l * 16 + t + 1)
                    if t >= 4:
                        act.wait_ge(ss_step, l * 4 + t // 4)
                    act.copy(KIT[t % 4][:, :], PB[:, t % 4, :]).then_inc(kit_e, 1)
                    if t == 11:
                        relu_group(0)
                relu_group(1)
                act.wait_ge(ss_mm, l + 1)
                for g in range(2):
                    e = act.activation(RELU_S[g][:, PAST:KEYS_S], PB[:, 0, RS * g:RS * g + RS], ACT.Relu)
                e.then_inc(ss_relu, 1)

                act.wait_ge(w_mm, l + 1)
                past = TKS[:, 0:PAST].rearrange("r (p j a) -> r a j p", j=KC, a=2)
                for par in range(2):
                    for jh in range(2):
                        e = act.copy(past[:, par, 4 * jh:4 * jh + 4, :],
                                     PS[par][0:RS, jh, :].rearrange("r (j p) -> r j p", j=4))
                e.then_inc(tks_past, 1)

                def plus_one(s, n, dst, c):
                    act.wait_ge(evac_done[s], n + 2)
                    apart(act, started)
                    v = dst[:, bass.ds(c, 1), :].rearrange("p o r -> p (o r)")
                    act.activation(v, v, ACT.Identity, bias=one[:, 0:1]).then_inc(inv_done, 1)

                def minus_exp(s, n, dst, c):
                    evac(s, n, lambda: act.activation(halves(dst[:, bass.ds(c, 1), :].rearrange("p o r -> p (o r)")),
                                                      PS[s][:, :, 0:RH], ACT.Exp, scale=-1.0))

                apart(act, started)
                with act.Fori(0, 4) as i:
                    for s in range(2):
                        n = l * USES[s] + i + phase_use(s, GA)
                        minus_exp(s, n, SG, i * 2 + s)
                        plus_one(s, n, SG, i * 2 + s)

                act.wait_ge(ue_init, l + 1)
                act.wait_ge(out_k[0], l * 48 + 48)
                act.wait_ge(out_k[1], l * 48 + 48)
                act.wait_ge(mp_ready, l + 1)
                apart(act, started)
                act.copy(QST[:, :], Q[:, 0, 0:RP]).then_inc(qst_done, 1)
                apart(act, started)
                with act.Fori(0, KC) as c:
                    H = l * HEADS + c

                    def gate_n(k):
                        s, u = gate_use(k, c)
                        return s, l * USES[s] + u

                    def high_only(k):
                        s, n = gate_n(k)
                        high(s, n + 1)

                    def h_rows():
                        s, n = gate_n(2)
                        act.wait_ge(evac_done[s], n)
                        s = gate_n(0)[0]
                        act.copy(UE[:, 2:2 + RH], PS[s][:, 0, 0:RH])
                        act.copy(UE[:, 2 + RH:2 + RP], PS[s][:, 1, 0:RP - RH])
                        return act.copy(UE[:, 2 + RP:UE_W].rearrange("p (b t) -> p b t", t=6)[:, :, 2:6],
                                        PS[s][:, 1, RP - RH:RH].rearrange("p (b t) -> p b t", t=NS))

                    def p_exp(i):
                        r = ORDER[i]
                        m = PTILES[r][1]
                        col = 512 * (0, 0, 1, 0, 1)[i]
                        act.wait_ge(lp_max, H * 5 + i + 1)
                        act.wait_ge(pp_t, H * 5 + i + (2 if i == 0 else 1))
                        act.activation(PP[i % 2][0:m, 0:KW[r]],
                                       PB[0:m].rearrange("p b k -> p (b k)")[:, col:col + KW[r]],
                                       ACT.Exp, bias=stp[0:m, i % 2, 0:1], scale=SC_HD,
                                       accum_out=stp[0:m, i % 2, 1:2]).then_inc(lp_exp, 1)

                    def p_norm(i):
                        r = ORDER[i]
                        m = PTILES[r][1]
                        act.wait_ge(lp_inv, H * 5 + i + 1)
                        act.mul(PP[i % 2][0:m, 0:KW[r]], PP[i % 2][0:m, 0:KW[r]], stp[0:m, i % 2, 3:4]
                                ).then_inc(pp_norm, 1)

                    def p_out(i):
                        c0, m = PTILES[ORDER[i]]
                        act.wait_ge(op_mm, H * 5 + i + 3)
                        apart(act, started)
                        act.copy(Q[:, bass.ds(c, 1), c0:c0 + m].rearrange("p o r -> p (o r)"),
                                 PB[:, 3, 0:m]).then_inc(op_e, 1)

                    p_exp(0)
                    p_norm(0)
                    s, n = gate_n(0)
                    evac(s, n, h_rows)
                    p_exp(1)
                    p_exp(2)
                    p_norm(1)
                    p_norm(2)
                    high_only(1)
                    p_out(0)
                    p_exp(3)
                    p_out(1)
                    p_norm(3)
                    high_only(2)
                    p_exp(4)
                    p_norm(4)
                    act.copy(QST[:, :], Q[:, bass.ds((c + 1) % KC, 1), 0:RP].rearrange("p o r -> p (o r)")).then_inc(qst_done, 1)
                    p_out(2)
                    s, n = gate_n(3)
                    minus_exp(s, n, BB, c)
                    p_out(3)
                    plus_one(s, n, BB, c)
                    p_out(4)
                act.wait_ge(cso_t, l + 1)
                act.wait_ge(out_small, l * 48 + 48)
                act.copy(CSN[:, 0, :], PB[:, 0, 0:P])
                act.copy(CSN[0:16, 1, :], PB[0:16, 0, P:2 * P]).then_inc(cso_e, 1)
                act.wait_ge(cso_e, l + 1)
                act.dma_start(a["o_cs"][bass.ds(l, 1)].rearrange("o b t (c d) -> (o b t c) d", d=P),
                              CSN[:, 0, :]).then_inc(out_c, 16)
                act.dma_start(a["o_c"][bass.ds(l, 1), 0].rearrange("o t (c d) -> (o t c) d", d=P),
                              CSN[0:16, 1, :]).then_inc(out_c, 16)
                apart(act, started)
                with act.Fori(0, 4) as i:
                    for s in range(2):
                        high(s, l * USES[s] + i + (phase_use(s, CONV) + 1))

                banks = [PS[0][:, 0, :], PS[0][:, 1, :], PS[1][:, 0, :]]
                act.wait_ge(qp_ready, l + 1)
                for g in range(2):
                    for t in range(0, 32, 2):
                        act.wait_ge(kt_t, l * 64 + 32 * g + t + 1)
                        if t >= 4:
                            act.wait_ge(kt_mm, l * 16 + 8 * g + t // 4)
                        act.copy(KTR[t % 4][:, :], banks[t % 3]).then_inc(kt_ea, 1)
                    act.wait_ge(ls_max, l * 2 + g + 1)
                    for c in (4, 0, 1, 2, 3):
                        src, w = (PB[:, c, :], 512) if c < 4 else (PS[1][:, 1, 0:RS], RS)
                        act.activation(PS_S[:, 512 * c:512 * c + w], src, ACT.Exp, bias=st[:, 5:6], scale=SC_HD,
                                       accum_out=st[:, 6 + c:7 + c]).then_inc(ls_exp, 1)
                    act.wait_ge(ot_t, l * 2 + g + 1)
                    for n in range(KVH):
                        col = RP + NS * 4 * g
                        e = act.copy(Q[:, GRP * n:GRP * n + GRP, col:col + 4 * NS].rearrange("p h (b s) -> p b h s", s=NS),
                                     PS[1][:, 1, P * n:P * n + P].rearrange("p (b h s) -> p b h s", b=4, s=NS)
                                     [:, :, GRP * n:GRP * n + GRP, :])
                    e.then_inc(ot_e, 1)

                for ph in (6, 7):
                    apart(act, started)
                    with act.Fori(0, 4) as i:
                        for s in range(2):
                            high(s, l * USES[s] + i + (phase_use(s, ph) + 1))

                def layer_norm(j):
                    for h in range(2):
                        act.wait_ge(ln_dev, l * 4 + 2 * j + h + 1)
                        act.activation(SQ[:, :, RH * h:RH * h + RH], X[:, :, RH * h:RH * h + RH], ACT.Square).then_inc(ln_sq, 1)
                    for h in range(2):
                        act.wait_ge(ln_var, l * 4 + 2 * j + h + 1)
                        act.activation(SD[:, RH * h:RH * h + RH], PS[1][:, h, 0:RH], ACT.Sqrt, bias=eps[:, 0:1]).then_inc(ln_sd, 1)
                    for c in range(KC + 1):
                        if c < KC:
                            act.wait_ge(ln_norm, l * 16 + 8 * j + c + 1)
                            act.activation(X[:, c, :], X[:, c, :], ACT.Identity,
                                           bias=PL[:, 16 * j + 8 + c:16 * j + 9 + c]).then_inc(ln_aff, 1)
                        if c > 0:
                            act.wait_ge(ln_aff, l * 16 + 8 * j + c)
                            act.copy(AXh[:, c - 1, :], X[:, c - 1, :]).then_inc(ln_hi, 1)

                layer_norm(0)
                apart(act, started)
                with act.Fori(0, NG) as g:
                    apart(act, started)
                    with act.Fori(0, 4) as i:
                        for s in range(2):
                            n = l * USES[s] + g * 8 + i + phase_use(s, MLP)
                            high(s, n + 1)
                            act.wait_ge(mm_done[s], n + 2)
                            act.wait_ge(a_ready, l * 72 + g * 8 + i * 2 + s + 39)
                            act.activation(halves(MT[s][:, :]), PS[s][:, :, 0:RH], ACT.Relu).then_inc(relu_h, 1)
                    apart(act, started)
                    with act.Fori(0, 4) as i:
                        for s in range(2):
                            high(s, l * USES[s] + g * 8 + i + (phase_use(s, MLP + 1) + 1))
                layer_norm(1)
                act.wait_ge(out_small, l * 48 + 48)
                act.wait_ge(out_v, l * 96 + 96)
                act.wait_ge(out_c, l * 32 + 32)

            for t, (c0, n) in enumerate([(16 + P * j, P) for j in range(4)] + [(RP, RS)]):
                act.wait_ge(y_t, t + 1)
                if t >= 2:
                    act.wait_ge(out_y[t % 2], 16 * (t // 2))
                act.copy(NAT[t % 2][0:n, :], PS[t % 2][0:n].rearrange("p b k -> p (b k)")).then_inc(y_e, 1)
                act.wait_ge(y_e, t + 1)
                dst = a["o_y"][0, P * t:P * t + P, :] if t < 4 else a["o_ys"].rearrange("b s d -> (b s) d")
                act.dma_start(dst, NAT[t % 2][0:n, :]).then_inc(out_y[t % 2], 16)
            act.wait_ge(out_y[0], 16 * 3)
            act.wait_ge(out_y[1], 16 * 2)
            for i in range(2):
                act.wait_ge(out_k[i], DEPTH * 48)

        def apart_drain(eng):
            apart(eng, started)
            return eng.drain()

        @block.vector
        def _(dve):
            own = Chain(dve, dve_own, started)

            for s in range(2):
                dve.sem_inc(evac_done[s], 1)
            for q in (lp_exp, pp_t, op_mm, op_e):
                dve.sem_inc(q, 2)
            dve.memset(ones[:, :], 1.0 / DM)
            dve.memset(eps[:, :], EPS)
            dve.memset(one[:, :], 1.0)
            dve.wait_ge(const_in, 16 * (NPG + 7 + 10))
            def half_rows():
                for h in range(2):
                    e = dve.tensor_scalar(IDXH[:, h, :], IDX[:, :], 2.0, float(h), ALU.mult, ALU.add)
                return e

            own.link(dve.tensor_scalar(IDX[:, :], PTB[:, :], float(PAGE // TPP), SEG[:, 0:1], ALU.mult, ALU.add))
            half_rows().then_inc(idx_ready, 1)
            dve.wait_ge(params_t, 1)
            own.link(dve.tensor_copy(PTT[:, :], PB[:, 0, 0:112]))
            dve.wait_ge(setup_e, 6)

            def split(hi, lo, src):
                own.link(dve.tensor_copy(hi, src))
                dve.tensor_tensor(lo, src, hi.bitcast(F32), ALU.subtract).then_inc(a_ready, 1)

            def chunk(t, c):
                return t[:, bass.ds(c, 1), :].rearrange("p o r -> p (o r)")

            def halves(v):
                return v.rearrange("p (h r) -> p h r", h=2)

            with own.fori(KC, 1) as c:
                split(chunk(AXh, c), chunk(AXl, c), chunk(X, c))

            with own.fori(DEPTH, LAYER_LINKS) as l:
                def use(s, n):
                    return l * USES[s] + n

                def rope(v, cos, sin, mask, tmp):
                    apart(dve, started)
                    own.link(dve.stream_shuffle(tmp, v, mask))
                    dve.tensor_tensor(v, v, cos, ALU.mult)
                    own.link(dve.tensor_tensor(tmp, tmp, sin, ALU.mult))
                    own.link(dve.tensor_tensor(v, v, tmp, ALU.add))

                own.link(dve.tensor_copy(PL[:, :], PTT[:, bass.ds(l * 56, 56)]))
                dve.wait_ge(tables_in, l * 64 + 64)
                for c in range(4):
                    dve.wait_ge(evac_done[c % 2], use(c % 2, c // 2) + 2)
                    rope(QI[:, c, :], ICOS[:, :], ISIN[:, :], rope_swap(IDX_ROT // 2), ROPE[:, :])
                for hp in range(2):
                    for par in range(2):
                        dve.tensor_copy(QS[ID * hp:ID * hp + ID, :, par::2, :],
                                        QI[ID * par:ID * par + ID, :, RP:R].rearrange("p c (b s) -> p b c s", s=NS))
                dve.wait_ge(evac_done[0], use(0, 2) + 2)
                rope(KI[0:ID, :], ICOS[0:ID, :], ISIN[0:ID, :], rope_swap(IDX_ROT // 2), ROPE[0:ID, :])
                dve.tensor_copy(KD[0:ID, :], KI[0:ID, :])
                dve.tensor_copy(KD[ID:P, :], KI[0:ID, :]).then_inc(ki_ready, 1)
                for h in range(KVH):
                    dve.wait_ge(evac_done[h], use(h, 3 - h) + 2)
                    rope(KT[0:32, h, :], QCOS[:, :], QSIN[:, :], rope_swap(ROT // 2), ROPE[0:32, :])
                apart_drain(dve).then_inc(kv_ready, 1)
                def in_parts(hi, lo, v):
                    own.link(dve.tensor_copy(hi, v))
                    return dve.tensor_tensor(lo, v, hi.bitcast(F32), ALU.subtract)

                in_parts(KDh[:, :], KDl[:, 0:RP], KD[:, 0:RP])
                for c in range(3):
                    e = in_parts(QIh[c][:, :], QIl[:, c, 0:RP], QI[:, c, 0:RP])
                e.then_inc(qi_split, 1)
                for c in range(KC):
                    s = c % 2
                    dve.wait_ge(evac_done[s], use(s, phase_use(s, QH) + c // 2 + 2))
                    rope(Q[0:32, c, :], QCOS[:, :], QSIN[:, :], rope_swap(ROT // 2), ROPE[0:32, :])
                apart_drain(dve).then_inc(q_ready, 1)
                dve.wait_ge(kv_e, l * 6 + 6)
                apart(dve, started)
                in_parts(QIh[3][:, :], QIl[:, 3, 0:RP], QI[:, 3, 0:RP]).then_inc(qi_split, 1)
                dve.wait_ge(ki_e, l + 1)
                dve.tensor_scalar(WKN[:, 1:4, ID:ID + IH], WKN[:, 1:4, ID:ID + IH], SC_WI, None, ALU.mult)
                own.link(dve.tensor_scalar(WKN[0:16, 4, ID:ID + IH], WKN[0:16, 4, ID:ID + IH], SC_WI, None, ALU.mult))
                dve.wait_ge(wi_mm, l + 1)
                dve.tensor_copy(SCT[:, :], PB[:, 1, P:2 * P])
                for g in range(2):
                    e = dve.scalar_tensor_tensor(WIB[:, g, :], PB[:, 1, 0:RS], SC_WI, pick[:, g, :], ALU.mult, ALU.mult)
                e.then_inc(wib_ready, 1)
                j = 0
                for r in range(1, 5):
                    c0, n = PTILES[r]
                    for h in range(IH):
                        dve.wait_ge(sc_relu, l * 32 + j + 1)
                        if j > 0:
                            dve.wait_ge(sc_acc, l * 32 + j)
                        w = WKN[0:n, r, ID + h:ID + h + 1]
                        if h == 0:
                            e = dve.tensor_scalar(TK[r][0:n, :], RELU_P[j % 2][0:n, 0:KW[r]], w, None, ALU.mult)
                        else:
                            e = dve.scalar_tensor_tensor(TK[r][0:n, :], RELU_P[j % 2][0:n, 0:KW[r]], w, TK[r][0:n, :],
                                                         ALU.mult, ALU.add)
                        e.then_inc(sc_acc, 1)
                        j += 1
                dve.wait_ge(sc_acc, l * 32 + 32)

                for r in range(1, 5):
                    n = PTILES[r][1]
                    e = dve.scalar_tensor_tensor(TK[r][0:n, P * r:P * r + n], caus[0:n, 0:n], NEG_KEY,
                                                 TK[r][0:n, P * r:P * r + n], ALU.mult, ALU.add)
                own.link(e)
                with own.fori(TOPK_P // 8, 8):
                    for r in range(1, 5):
                        n = PTILES[r][1]
                        own.wait(behind=3)
                        own.count(dve.max(top[0:n, r - 1, :], TK[r][0:n, :]))
                    for r in range(1, 5):
                        n = PTILES[r][1]
                        own.wait(behind=3)
                        own.count(dve.match_replace(TK[r][0:n, :], top[0:n, r - 1, :], TK[r][0:n, :], NEG_TAKEN))
                own.wait()
                dve.wait_ge(kv_e, l * 6 + 6)
                for r in range(1, 5):
                    n = PTILES[r][1]
                    e = dve.tensor_scalar(MP[r][0:n, :], TK[r][0:n, :], NEG_CUT, NEG_MASK, ALU.is_gt, ALU.mult)
                e.then_inc(mp_ready, 1)
                dve.wait_ge(w_mm, l + 1)
                dve.wait_ge(tks_past, l + 1)
                dve.scalar_tensor_tensor(TKS[:, PAST:KEYS_S], newok[:, :], NEG_KEY, PB[0:RS, 1, 0:RS],
                                         ALU.mult, ALU.add).then_inc(tks_ready, 1)
                dve.wait_ge(tks_ready, l + 1)
                dve.memset(UE[:, 0:2], 0.0).then_inc(ue_init, 1)
                past_t = UE[:, 2 + RP:UE_W].rearrange("p (b t) -> p b t", t=6)
                state = SCT[:, :].rearrange("p (b t c) -> p b t c", b=NB, c=KC)

                def s_top():
                    own.link(dve.max(top[0:RS, 0, :], TKS[:, :]), alone=True)

                def s_take():
                    own.link(dve.match_replace(TKS[:, :], top[0:RS, 0, :], TKS[:, :], NEG_TAKEN), alone=True)

                with own.fori(4, 2) as i:
                    s_top()
                    s_take()

                with own.fori(KC, HEAD_LINKS) as c:
                    H = l * HEADS + c

                    def gate_n(k):
                        s, u = gate_use(k, c)
                        return s, l * USES[s] + u

                    def p_max(i):
                        r = ORDER[i]
                        m = PTILES[r][1]
                        col = 512 * (0, 0, 1, 0, 1)[i]
                        dve.wait_ge(lp_mm, H * 5 + i + 1)
                        dve.wait_ge(lp_exp, H * 5 + i + (2 if i == 0 else 1))
                        own.link(dve.tensor_reduce(
                            stp[0:m, i % 2, 2:3],
                            PB[0:m].rearrange("p b k -> p (b k)")[:, col:col + KW[r]], AX_X, ALU.max))
                        dve.tensor_scalar(stp[0:m, i % 2, 0:1], stp[0:m, i % 2, 2:3], -SC_HD, None, ALU.mult
                                          ).then_inc(lp_max, 1)

                    def p_inv(i):
                        m = PTILES[ORDER[i]][1]
                        dve.wait_ge(lp_exp, H * 5 + i + 3)
                        dve.reciprocal(stp[0:m, i % 2, 3:4], stp[0:m, i % 2, 1:2]).then_inc(lp_inv, 1)

                    def p_turned(i):
                        r = ORDER[i]
                        m = PTILES[r][1]
                        full = (KW[r] // P) * m
                        dve.wait_ge(pp_t, H * 5 + i + 3)
                        dve.wait_ge(op_mm, H * 5 + i + (2 if i == 0 else 1))
                        if KW[r] % P:
                            dve.tensor_copy(PPT[i % 2][0:KW[r] % P, full:full + m], PB[0:KW[r] % P, 2, full:full + m])
                        dve.tensor_copy(PPT[i % 2][:, 0:full], PB[:, 2, 0:full]).then_inc(pp_e, 1)

                    def gate_c():
                        s, n = gate_n(1)
                        dve.wait_ge(evac_done[gate_n(0)[0]], gate_n(0)[1] + 2)
                        dve.wait_ge(mm_done[s], n + 2)
                        for u, z in ((UE[:, 2:2 + RH], PS[s][:, 0, 0:RH]),
                                     (UE[:, 2 + RH:2 + RP], PS[s][:, 1, 0:RP - RH]),
                                     (past_t[:, :, 2:6], PS[s][:, 1, RP - RH:RH].rearrange("p (b t) -> p b t", t=NS))):
                            e = dve.tensor_tensor(u, z, u, ALU.mult)
                        e.then_inc(evac_done[s], 1)
                        dve.wait_ge(evac_done[s], n + 2)
                        dve.tensor_copy(CSO[:, 16:18, bass.ds(c, 1)].rearrange("p t o -> p (t o)"), UE[:, RP:RP + 2])
                        dve.tensor_copy(CSO[:, 0:16, bass.ds(c, 1)].rearrange("p (b t) o -> p b (t o)", t=2),
                                        past_t[:, :, 4:6])
                        own.link(dve.tensor_copy(past_t[:, :, 0:2],
                                                 state[:, :, :, bass.ds(c, 1)].rearrange("p b t o -> p b (t o)")))

                    def short_conv():
                        w = [PL[:, bass.ds(c + (32 + KC * t), 1)] for t in range(CW)]
                        cys = CY[:, RP:R].rearrange("p (b t) -> p b t", t=NS)
                        dve.tensor_scalar(CY[:, 0:RP], UE[:, 0:RP], w[0], None, ALU.mult)
                        own.link(dve.tensor_scalar(cys, past_t[:, :, 0:NS], w[0], None, ALU.mult))
                        for t in range(1, CW):
                            dve.scalar_tensor_tensor(CY[:, 0:RP], UE[:, t:t + RP], w[t], CY[:, 0:RP], ALU.mult, ALU.add)
                            own.link(dve.scalar_tensor_tensor(cys, past_t[:, :, t:t + NS], w[t], cys, ALU.mult, ALU.add))

                    def gate_b():
                        s, n = gate_n(2)
                        dve.wait_ge(mm_done[s], n + 2)
                        dve.tensor_tensor(halves(CY[:, :]), PS[s][:, :, 0:RH], halves(CY[:, :]), ALU.mult
                                          ).then_inc(evac_done[s], 1)
                        dve.wait_ge(evac_done[s], n + 2)
                        split(chunk(AHh, c), chunk(AHl, c), CY[:, :])

                    p_max(0)
                    s_top()
                    p_inv(0)
                    s_take()
                    p_turned(0)
                    p_max(1)
                    p_max(2)
                    p_inv(1)
                    p_inv(2)
                    s_top()
                    s_take()
                    p_turned(1)
                    p_max(3)
                    p_turned(2)
                    gate_c()
                    p_inv(3)
                    s_top()
                    short_conv()
                    apart(dve, started)
                    s_take()
                    p_max(4)
                    p_turned(3)
                    p_inv(4)
                    gate_b()
                    p_turned(4)
                apart_drain(dve).then_inc(cso_ready, 1)
                for s in range(2):
                    dve.wait_ge(evac_done[s], use(s, phase_use(s, CONV) + 1))
                own.link(dve.memset(QP[:, :, :, :, :], 0.0))
                for n in range(KVH):
                    e = dve.tensor_copy(QP[:, :, n, GRP * n:GRP * n + GRP, :],
                                        Q[:, GRP * n:GRP * n + GRP, RP:R].rearrange("p h (b s) -> p b h s", s=NS))
                e.then_inc(qp_ready, 1)

                def sigmoid(v):
                    own.link(dve.reciprocal(v, v))

                dve.wait_ge(inv_done, l * 16 + 16)
                with own.fori(4, 4) as i:
                    s_top()
                    s_take()
                    for s in range(2):
                        sigmoid(chunk(BB, i * 2 + s))
                        n = l * USES[s] + i + phase_use(s, CONV)
                        dve.wait_ge(mm_done[s], n + 2)
                        bb = halves(chunk(BB, i * 2 + s))
                        dve.tensor_tensor(bb, PS[s][:, :, 0:RH], bb, ALU.mult).then_inc(evac_done[s], 1)
                dve.tensor_scalar(MS[:, 0:PAST].rearrange("r (i p) -> r i p", p=P),
                                  TKS[:, 0:PAST].rearrange("r (p i) -> r i p", p=P), NEG_CUT, NEG_MASK,
                                  ALU.is_gt, ALU.mult)
                dve.tensor_scalar(MS[:, PAST:KEYS_S], TKS[:, PAST:KEYS_S], NEG_CUT, NEG_MASK,
                                  ALU.is_gt, ALU.mult).then_inc(masks_ready, 1)

                banks = [PS[0][:, 0, :], PS[0][:, 1, :], PS[1][:, 0, :]]

                def split_heads(c0, c1):
                    with own.fori(c1 - c0, 1) as c:
                        hi, lo, q = (chunk(t, c + c0)[:, 0:RP] for t in (AXh, AXl, Q))
                        own.link(dve.tensor_copy(hi, q))
                        dve.tensor_tensor(lo, q, hi.bitcast(F32), ALU.subtract)

                for g in range(2):
                    for t in range(1, 32, 2):
                        dve.wait_ge(kt_t, l * 64 + 32 * g + t + 1)
                        if t >= 4:
                            dve.wait_ge(kt_mm, l * 16 + 8 * g + t // 4)
                        dve.tensor_copy(KTR[t % 4][:, :], banks[t % 3]).then_inc(kt_ed, 1)
                        if g == 1 and t % 8 == 1:
                            own.link(dve.reciprocal(SG[:, 4 + t // 8, :], SG[:, 4 + t // 8, :]))
                        if t in (11, 19, 27):
                            c = (t - 11) // 8
                            dve.wait_ge(ls_mm, l * 10 + 5 * g + (c if c < 2 else 3) + 1)
                            dve.reduce_max(st[:, c:c + 1], PB[:, c, :], AX_X)
                            if c == 2:
                                dve.reduce_max(st[:, 4:5], PS[1][:, 1, 0:RS], AX_X)
                    dve.wait_ge(ls_mm, l * 10 + 5 * g + 5)
                    own.link(dve.reduce_max(st[:, 3:4], PB[:, 3, :], AX_X))
                    own.link(dve.reduce_max(st[:, 13:14], st[:, 0:5], AX_X))
                    dve.tensor_scalar(st[:, 5:6], st[:, 13:14], -SC_HD, None, ALU.mult).then_inc(ls_max, 1)
                    for c in range(5):
                        dve.wait_ge(pt_t, l * 10 + 5 * g + c + 1)
                        if c == 4:
                            dve.wait_ge(pv_mm, l * 10 + 5 * g + 1)
                        w, kn = (512, P) if c < 4 else (P, RS)
                        dve.tensor_copy(KTR[c % 4][0:kn, 0:w], banks[c % 3][0:kn, 0:w]).then_inc(pt_e, 1)
                    dve.wait_ge(ls_exp, l * 10 + 5 * g + 5)
                    own.link(dve.reduce_sum(st[:, 11:12], st[:, 6:11], AX_X))
                    own.link(dve.reciprocal(st[:, 12:13], st[:, 11:12]))
                    if g == 1:
                        dve.wait_ge(pv_mm, l * 10 + 7)
                        split_heads(0, 3)
                    dve.wait_ge(pv_mm, l * 10 + 5 * g + 5)
                    dve.tensor_scalar(O_S[:, :], PS[1][:, 1, KV_W:2 * KV_W], st[:, 12:13], None, ALU.mult
                                      ).then_inc(os_e, 1)
                    if g == 0:
                        with own.fori(4, 1) as c:
                            sigmoid(chunk(SG, c))
                split_heads(3, KC)
                dve.wait_ge(ot_e, l * 2 + 2)
                own.link(dve.tensor_copy(AXh[:, :, RP:R], Q[:, :, RP:R]))
                dve.tensor_tensor(AXl[:, :, RP:R], Q[:, :, RP:R], AXh[:, :, RP:R].bitcast(F32), ALU.subtract
                                  ).then_inc(a_ready, KC)
                with own.fori(4, 2 * 2) as i:
                    for s in range(2):
                        n = l * USES[s] + i + phase_use(s, AO)
                        dve.wait_ge(mm_done[s], n + 2)
                        dve.tensor_tensor(halves(MT[s][:, :]), PS[s][:, :, 0:RH], halves(chunk(SG, i * 2 + s)), ALU.mult
                                          ).then_inc(evac_done[s], 1)
                        dve.wait_ge(evac_done[s], n + 2)
                        own.link(dve.tensor_tensor(MT[s][:, :], MT[s][:, :], chunk(BB, i * 2 + s), ALU.add))
                        split(chunk(AHh, i * 2 + s), chunk(AHl, i * 2 + s), MT[s][:, :])
                own.link(dve.memset(XS[:, :], 0.0))
                with own.fori(4, 2) as i:
                    for s in range(2):
                        n = l * USES[s] + i + phase_use(s, WO)
                        dve.wait_ge(mm_done[s], n + 2)
                        x = halves(chunk(X, i * 2 + s))
                        dve.scalar_tensor_tensor(x, x, ALPHA, PS[s][:, :, 0:RH], ALU.mult, ALU.add
                                                 ).then_inc(evac_done[s], 1)
                        dve.wait_ge(evac_done[s], n + 2)
                        own.link(dve.tensor_tensor(XS[:, :], XS[:, :], chunk(X, i * 2 + s), ALU.add))

                def layer_norm(j):
                    apart_drain(dve).then_inc(xs_ready, 1)
                    for h in range(2):
                        dve.wait_ge(ln_sum, l * 4 + 2 * j + h + 1)
                        x = X[:, :, RH * h:RH * h + RH]
                        dve.tensor_tensor(x, x, PS[0][:, h, 0:RH].unsqueeze(1).to_broadcast([P, KC, RH]), ALU.subtract
                                          ).then_inc(ln_dev, 1)
                    for h in range(2):
                        dve.wait_ge(ln_sq, l * 4 + 2 * j + h + 1)
                        dve.reduce_sum(SS[:, RH * h:RH * h + RH],
                                       SQ[:, :, RH * h:RH * h + RH].rearrange("p c r -> p r c"), AX_X).then_inc(ln_red, 1)
                    for h in range(2):
                        dve.wait_ge(ln_sd, l * 4 + 2 * j + h + 1)
                        own.link(dve.reciprocal(RSTD[:, RH * h:RH * h + RH], SD[:, RH * h:RH * h + RH]))
                    for c in range(KC + 2):
                        if c < KC:
                            dve.scalar_tensor_tensor(X[:, c, :], X[:, c, :], PL[:, 16 * j + c:16 * j + c + 1], RSTD[:, :],
                                                     ALU.mult, ALU.mult).then_inc(ln_norm, 1)
                        if c > 1:
                            dve.wait_ge(ln_hi, l * 16 + 8 * j + c - 1)
                            dve.tensor_tensor(AXl[:, c - 2, :], X[:, c - 2, :], AXh[:, c - 2, :].bitcast(F32),
                                              ALU.subtract).then_inc(a_ready, 1)

                layer_norm(0)
                dve.wait_ge(a_ready, l * 72 + 40)
                own.link(dve.tensor_scalar(X[:, :, :].rearrange("p c r -> p (c r)"), X[:, :, :].rearrange("p c r -> p (c r)"),
                                           ALPHA, None, ALU.mult))
                with own.fori(NG, 4 * 2 * 1 + 1 + 4 * 2 * 1) as g:
                    with own.fori(4, 2 * 1) as i:
                        for s in range(2):
                            n = l * USES[s] + g * 8 + i + phase_use(s, MLP)
                            dve.wait_ge(relu_h, l * 32 + g * 8 + i * 2 + s + 1)
                            dve.scalar_tensor_tensor(halves(MT[2 + s][:, :]), PS[s][:, :, 0:RH], 0.0, halves(MT[s][:, :]),
                                                     ALU.max, ALU.mult).then_inc(evac_done[s], 1)
                            dve.wait_ge(evac_done[s], n + 2)
                            split(chunk(AHh, i * 2 + s), chunk(AHl, i * 2 + s), MT[2 + s][:, :])
                    own.link(dve.memset(XS[:, :], 0.0))
                    with own.fori(4, 2 * 1) as i:
                        for s in range(2):
                            n = l * USES[s] + g * 8 + i + phase_use(s, MLP + 1)
                            dve.wait_ge(mm_done[s], n + 2)
                            dve.wait_ge(evac_done[s], n + 1)
                            x = halves(chunk(X, i * 2 + s))
                            dve.tensor_tensor(x, x, PS[s][:, :, 0:RH], ALU.add).then_inc(evac_done[s], 1)
                            dve.wait_ge(evac_done[s], n + 2)
                            own.link(dve.tensor_tensor(XS[:, :], XS[:, :], chunk(X, i * 2 + s), ALU.add))
                own.link(dve.tensor_scalar(IDX[:, :], IDX[:, :], float(n_rows), None, ALU.add))
                half_rows().then_inc(idx_ready, 1)
                layer_norm(1)


def constants():
    import numpy as np

    f = np.float32
    pos = np.concatenate([np.arange(RP), np.tile(PAST + np.arange(NS), NB)]).astype(f)

    def table(rot, width):
        half = rot // 2
        inv = (f(500000.0) ** (-np.arange(half, dtype=f) * f(2.0) / f(rot))).astype(f)
        ang = (pos[None, :] * inv[:, None]).astype(f)
        cos, sin = np.ones((width, R), f), np.zeros((width, R), f)
        cos[:half] = cos[half:rot] = np.cos(ang)
        sin[:half], sin[half:rot] = -np.sin(ang), np.sin(ang)
        return cos, sin

    icos, isin = table(IDX_ROT, ID)
    qcos, qsin = table(ROT, 32)
    q = np.arange(P)
    sel = np.zeros((RS, 2, P), f)
    pick = np.zeros((P, 2, RS), f)
    for b in range(NB):
        for h in range(HEADS):
            for s in range(NS):
                row = 32 * (b % 4) + NS * h + s
                sel[NS * b + s, b // 4, row] = 1
                pick[row, b // 4, NS * b + s] = 1
    expand = np.zeros((P, P), f)
    for h in range(IH):
        expand[ID + h] = (q % 32) // NS == h
    r = np.arange(RS)
    newok = ~((r[:, None] // NS == r[None, :] // NS) & (r[None, :] <= r[:, None]))
    return {
        "c_ident": np.eye(P, dtype=f), "c_caus": (q[None, :] > q[:, None]).astype(f), "c_expand": expand,
        "c_pick": pick, "c_newok": newok.astype(f), "c_seg": (q % (PAGE // TPP)).astype(f)[:, None], "c_sel": sel,
        "c_icos": np.concatenate([icos, icos]), "c_isin": np.concatenate([isin, isin]), "c_qcos": qcos, "c_qsin": qsin,
    }


_INS = ["x_prompt", "x_sample", "cache_k", "cache_v", "cache_idx_k", "state_conv", "page_table", "meta_tokens",
        "w_in", "conv_w", "w_attn_out", "w_conv_out", "w_o", "ln1_g", "ln1_b", "w_up", "w_down", "ln2_g", "ln2_b"]
_OUTS = [("o_y", (1, SEQ, DM)), ("o_ys", (NB, NS, DM)), ("o_k", (DEPTH, 1, RP, KVH, HD)), ("o_v", (DEPTH, 1, RP, KVH, HD)),
         ("o_ik", (DEPTH, 1, RP, ID)), ("o_c", (DEPTH, 1, CW - 1, DM)), ("o_ks", (DEPTH, NB, NS, KVH, HD)),
         ("o_vs", (DEPTH, NB, NS, KVH, HD)), ("o_iks", (DEPTH, NB, NS, ID)), ("o_cs", (DEPTH, NB, CW - 1, DM))]


def kernel(**inputs):
    import numpy as _np
    import concourse.bacc as _bacc
    from concourse import mybir as _mybir
    from concourse.bass_utils import run_bass_kernel_spmd as _run

    nc = _bacc.Bacc("TRN2", target_bir_lowering=False, num_devices=1)
    arrays, aps = {}, {}
    data = {n: _np.ascontiguousarray(inputs[n]) for n in _INS}
    data.update(constants())
    for name, v in data.items():
        arrays[f"in_{name}_dram"] = v
        aps[name] = nc.dram_tensor(f"in_{name}_dram", v.shape, _mybir.dt.from_np(v.dtype), kind="ExternalInput").ap()
    for name, shape in _OUTS:
        aps[name] = nc.dram_tensor(f"{name}_dram", shape, F32, kind="ExternalOutput").ap()
    trunk_program(nc, aps)
    r = _run(nc, [arrays], core_ids=[0])
    return tuple(r.results[0][f"{name}_dram"] for name, _ in _OUTS)
```
